# Optimizing a Trainium2 kernel written in Bass

```python
import math
import jax, jax.numpy as jnp
from jax import lax
import numpy as np

D_MODEL = 2048
BATCH = 1
SEQ = 512
DEPTH = 1

ATTN_HEADS = 8
ATTN_QK_DIM = 64
ATTN_V_DIM = 2 * ATTN_QK_DIM
ATTN_QK_WIDTH = ATTN_HEADS * 2 * ATTN_QK_DIM
ATTN_WIDTH = ATTN_HEADS * ATTN_V_DIM
Q_BLOCK = 128
MLSTM_HEADS = 4
MLSTM_QK_DIM = 128
MLSTM_V_DIM = 256
MLSTM_QK_WIDTH = MLSTM_HEADS * MLSTM_QK_DIM
MLSTM_WIDTH = MLSTM_HEADS * MLSTM_V_DIM
CONV_WIDTH = 4
CHUNK = 64
N_MEM = 256
CROSS_HEADS = 4
CROSS_HEAD_DIM = 128
CROSS_WIDTH = CROSS_HEADS * CROSS_HEAD_DIM
D_FF = 4 * D_MODEL
EPS = 1e-6
IN_WIDTHS = (ATTN_QK_WIDTH, ATTN_QK_WIDTH, ATTN_WIDTH, 2 * MLSTM_QK_WIDTH, MLSTM_WIDTH, MLSTM_WIDTH, MLSTM_HEADS, MLSTM_HEADS, D_MODEL, D_MODEL)
IN_WIDTH = sum(IN_WIDTHS)

kernel_name = "hybrid_diffattn_mlstm_gated_block"

def rms_norm(x, g):
    xf = x.astype(jnp.float32)
    y = xf * lax.rsqrt(jnp.mean(xf * xf, axis=-1, keepdims=True) + EPS)
    return (y * g.astype(jnp.float32)).astype(x.dtype)

def split_cols(z):
    idx, acc = [], 0
    for w in IN_WIDTHS[:-1]:
        acc += w
        idx.append(acc)
    return jnp.split(z, idx, axis=-1)

def causal_conv(u, w, b):
    c = u.shape[-1]
    out = lax.conv_general_dilated(u, w[:, None, :].astype(u.dtype), window_strides=(1,), padding=[(CONV_WIDTH - 1, 0)], dimension_numbers=('NWC', 'WIO', 'NWC'), feature_group_count=c)
    return out + b

def diff_attention(q, k, v, lam, slopes):
    b_, s_ = q.shape[:2]
    nb = s_ // Q_BLOCK
    scale = ATTN_QK_DIM ** -0.5
    q_blocks = q.reshape(b_, nb, Q_BLOCK, ATTN_HEADS, 2, ATTN_QK_DIM).swapaxes(0, 1)
    starts = jnp.arange(nb, dtype=jnp.int32) * Q_BLOCK
    k_pos = jnp.arange(s_, dtype=jnp.int32)
    v32 = v.astype(jnp.float32)

    def block(args):
        q_blk, start = args
        q_pos = start + jnp.arange(Q_BLOCK, dtype=jnp.int32)
        dist = q_pos[:, None] - k_pos[None, :]
        bias = -slopes[:, None, None] * dist.astype(jnp.float32)
        s = jnp.einsum('bqhmd,bkhmd->bhmqk', q_blk, k).astype(jnp.float32) * scale + bias[None, :, None]
        s = jnp.where(dist >= 0, s, -jnp.inf)
        p = jax.nn.softmax(s, axis=-1)
        w = p[:, :, 0] - lam * p[:, :, 1]
        return jnp.einsum('bhqk,bkhd->bqhd', w, v32)

    out = lax.map(block, (q_blocks, starts))
    return out.swapaxes(0, 1).reshape(b_, s_, ATTN_HEADS, ATTN_V_DIM)

def mlstm(q, k, v, i_pre, f_pre):
    b_, s_, h_, dk = q.shape
    dv = v.shape[-1]
    nc = s_ // CHUNK

    def chunks(t):
        return t.astype(jnp.float32).swapaxes(1, 2).reshape(b_, h_, nc, CHUNK, *t.shape[3:])

    q = chunks(q)
    k = chunks(k) * (dk ** -0.5)
    v = chunks(v)
    log_i = chunks(i_pre)
    log_f = jax.nn.log_sigmoid(chunks(f_pre))
    b = jnp.cumsum(log_f, axis=-1)
    g = b[..., -1]
    causal = jnp.tril(jnp.ones((CHUNK, CHUNK), dtype=bool))
    d = jnp.where(causal, b[..., :, None] - b[..., None, :] + log_i[..., None, :], -jnp.inf)
    a = g[..., None] - b + log_i
    m_loc = jnp.max(a, axis=-1)
    wa = jnp.exp(a - m_loc[..., None])
    c_loc = jnp.einsum('bhcsk,bhcsv->bhckv', wa[..., None] * k, v)
    n_loc = jnp.einsum('bhcs,bhcsk->bhck', wa, k)

    def step(carry, inp):
        c, n, m = carry
        c_l, n_l, m_l, g_c = inp
        m_new = jnp.maximum(g_c + m, m_l)
        a_old = jnp.exp(g_c + m - m_new)
        a_new = jnp.exp(m_l - m_new)
        c_new = a_old[..., None, None] * c + a_new[..., None, None] * c_l
        n_new = a_old[..., None] * n + a_new[..., None] * n_l
        return (c_new, n_new, m_new), (c, n, m)

    init = (jnp.zeros((b_, h_, dk, dv), jnp.float32), jnp.zeros((b_, h_, dk), jnp.float32), jnp.zeros((b_, h_), jnp.float32))
    xs = (jnp.moveaxis(c_loc, 2, 0), jnp.moveaxis(n_loc, 2, 0), jnp.moveaxis(m_loc, 2, 0), jnp.moveaxis(g, 2, 0))
    _, (c_prev, n_prev, m_prev) = lax.scan(step, init, xs)
    c_prev = jnp.moveaxis(c_prev, 0, 2)
    n_prev = jnp.moveaxis(n_prev, 0, 2)
    m_prev = jnp.moveaxis(m_prev, 0, 2)

    m_inter = b + m_prev[..., None]
    m_j = jnp.maximum(m_inter, jnp.max(d, axis=-1))
    w_inter = jnp.exp(m_inter - m_j)
    qk = jnp.einsum('bhcjd,bhcsd->bhcjs', q, k) * jnp.exp(d - m_j[..., None])
    num = w_inter[..., None] * jnp.einsum('bhcjk,bhckv->bhcjv', q, c_prev) + jnp.einsum('bhcjs,bhcsv->bhcjv', qk, v)
    den = w_inter * jnp.einsum('bhcjk,bhck->bhcj', q, n_prev) + jnp.sum(qk, axis=-1)
    h = num / jnp.maximum(jnp.abs(den), jnp.exp(-m_j))[..., None]
    return h.reshape(b_, h_, s_, dv).swapaxes(1, 2)

def setup_inputs(seed: int = 0) -> dict:
    key = jax.random.key(seed)
    ks = iter(jax.random.split(key, 40))
    f32 = jnp.float32

    def normal(shape, scale):
        return jax.random.normal(next(ks), shape, f32) * scale

    def gain(shape):
        return 1.0 + normal(shape, 0.02)

    L = DEPTH
    return {
        "x": normal((BATCH, SEQ, D_MODEL), 1.0),
        "mem": normal((BATCH, N_MEM, D_MODEL), 1.0),
        "norm_mix": gain((L, D_MODEL)),
        "w_in": normal((L, D_MODEL, IN_WIDTH), D_MODEL ** -0.5),
        "b_igate": normal((L, MLSTM_HEADS), 0.1),
        "b_fgate": jnp.broadcast_to(jnp.linspace(3.0, 6.0, MLSTM_HEADS, dtype=f32), (L, MLSTM_HEADS)) + normal((L, MLSTM_HEADS), 0.1),
        "conv_w": normal((L, CONV_WIDTH, 2 * MLSTM_QK_WIDTH), CONV_WIDTH ** -0.5),
        "conv_b": normal((L, 2 * MLSTM_QK_WIDTH), 0.02),
        "lam_q1": normal((L, ATTN_QK_DIM), 0.1),
        "lam_k1": normal((L, ATTN_QK_DIM), 0.1),
        "lam_q2": normal((L, ATTN_QK_DIM), 0.1),
        "lam_k2": normal((L, ATTN_QK_DIM), 0.1),
        "attn_norm": gain((L, ATTN_V_DIM)),
        "mlstm_norm": gain((L, MLSTM_WIDTH)),
        "w_attn_br": normal((L, ATTN_WIDTH, D_MODEL), ATTN_WIDTH ** -0.5),
        "w_mlstm_br": normal((L, MLSTM_WIDTH, D_MODEL), MLSTM_WIDTH ** -0.5),
        "w_out": normal((L, D_MODEL, D_MODEL), D_MODEL ** -0.5),
        "norm_cross": gain((L, D_MODEL)),
        "norm_mem": gain((L, D_MODEL)),
        "w_cq": normal((L, D_MODEL, CROSS_WIDTH), D_MODEL ** -0.5),
        "w_ckv": normal((L, D_MODEL, 2 * CROSS_WIDTH), D_MODEL ** -0.5),
        "w_co": normal((L, CROSS_WIDTH, D_MODEL), CROSS_WIDTH ** -0.5),
        "norm_mlp": gain((L, D_MODEL)),
        "w_up": normal((L, D_MODEL, D_FF), D_MODEL ** -0.5),
        "w_down": normal((L, D_FF, D_MODEL), D_FF ** -0.5),
        "norm_final": gain((D_MODEL,)),
    }

def reference(x, mem, norm_mix, w_in, b_igate, b_fgate, conv_w, conv_b, lam_q1, lam_k1, lam_q2, lam_k2, attn_norm, mlstm_norm, w_attn_br, w_mlstm_br, w_out, norm_cross, norm_mem, w_cq, w_ckv, w_co, norm_mlp, w_up, w_down, norm_final):
    b_, s_, _ = x.shape
    n_mem = mem.shape[1]
    slopes = jnp.exp2(-8.0 * jnp.arange(1, ATTN_HEADS + 1, dtype=jnp.float32) / ATTN_HEADS)
    for l in range(DEPTH):
        h = rms_norm(x, norm_mix[l])
        z = h @ w_in[l]
        aq, ak, av, mqk, mv, mo, mi, mf, ga, gm = split_cols(z)

        lam_init = 0.8 - 0.6 * math.exp(-0.3 * l)
        lam = (jnp.exp(jnp.dot(lam_q1[l], lam_k1[l]).astype(jnp.float32))
               - jnp.exp(jnp.dot(lam_q2[l], lam_k2[l]).astype(jnp.float32)) + lam_init)
        att = diff_attention(aq.reshape(b_, s_, ATTN_HEADS, 2, ATTN_QK_DIM),
                             ak.reshape(b_, s_, ATTN_HEADS, 2, ATTN_QK_DIM),
                             av.reshape(b_, s_, ATTN_HEADS, ATTN_V_DIM), lam, slopes)
        att = rms_norm(att, attn_norm[l]) * (1.0 - lam_init)
        att = att.reshape(b_, s_, ATTN_WIDTH).astype(x.dtype)

        mqk = jax.nn.silu(causal_conv(mqk, conv_w[l], conv_b[l]))
        mq, mk = jnp.split(mqk, 2, axis=-1)
        hm = mlstm(mq.reshape(b_, s_, MLSTM_HEADS, MLSTM_QK_DIM),
                   mk.reshape(b_, s_, MLSTM_HEADS, MLSTM_QK_DIM),
                   mv.reshape(b_, s_, MLSTM_HEADS, MLSTM_V_DIM),
                   mi + b_igate[l], mf + b_fgate[l])
        hm = rms_norm(hm, mlstm_norm[l].reshape(MLSTM_HEADS, MLSTM_V_DIM))
        hm = (hm.reshape(b_, s_, MLSTM_WIDTH) * jax.nn.sigmoid(mo.astype(jnp.float32))).astype(x.dtype)

        y = jax.nn.sigmoid(ga) * (att @ w_attn_br[l]) + jax.nn.sigmoid(gm) * (hm @ w_mlstm_br[l])
        x = x + y @ w_out[l]

        hc = rms_norm(x, norm_cross[l])
        mn = rms_norm(mem, norm_mem[l])
        cq = (hc @ w_cq[l]).reshape(b_, s_, CROSS_HEADS, CROSS_HEAD_DIM)
        ck, cv = jnp.split(mn @ w_ckv[l], 2, axis=-1)
        ck = ck.reshape(b_, n_mem, CROSS_HEADS, CROSS_HEAD_DIM)
        cv = cv.reshape(b_, n_mem, CROSS_HEADS, CROSS_HEAD_DIM)
        cs = jnp.einsum('bqhd,bkhd->bhqk', cq, ck).astype(jnp.float32) * (CROSS_HEAD_DIM ** -0.5)
        cp = jax.nn.softmax(cs, axis=-1)
        co = jnp.einsum('bhqk,bkhd->bqhd', cp, cv.astype(jnp.float32)).reshape(b_, s_, CROSS_WIDTH).astype(x.dtype)
        x = x + co @ w_co[l]

        hf = rms_norm(x, norm_mlp[l])
        x = x + jnp.square(jax.nn.relu(hf @ w_up[l])) @ w_down[l]
    return rms_norm(x, norm_final)


_drawn_inputs = setup_inputs


def setup_inputs(seed=0):
    import zlib

    import numpy as np

    out = dict(_drawn_inputs(seed))
    spreads = {}
    factors = {'norm_mix': 3.127,
     'b_igate': 64.0,
     'conv_b': 8.0,
     'lam_k1': 8.0,
     'lam_q2': 8.0,
     'attn_norm': 7.312,
     'mlstm_norm': 8.0,
     'norm_cross': 8.0,
     'norm_mem': 8.0,
     'norm_mlp': 9.848,
     'norm_final': 7.45}
    for name, (base, spread) in spreads.items():
        noise = np.random.default_rng([zlib.crc32(name.encode()), seed]).standard_normal(out[name].shape)
        drawn = base * np.exp(spread * noise) if base else spread * noise
        out[name] = __import__('jax').numpy.asarray(drawn.astype(out[name].dtype))
    for name, factor in factors.items():
        out[name] = (out[name] * factor).astype(out[name].dtype)
    return out
```

```python
import math
from contextlib import ExitStack

import numpy as np

import concourse.bass as bass
from concourse import mybir

F32 = mybir.dt.float32
F32R = mybir.dt.float32r
ACT = mybir.ActivationFunctionType
ALU = mybir.AluOpType
AX = mybir.AxisListType.X

P = 128
SEQ = 512
D = 2048
NT = SEQ // P
KD = D // P
MEM = 256
MT = MEM // P
HEADS = 8
QK = 64
MH = 4
MV = 256
CH = 4
CONV = 4
D_FF = 4 * D
EPS = 1e-6
LAM_INIT = 0.8 - 0.6 * math.exp(-0.3 * 0)
BLK = 512
GR = 4
FF_CHUNK = 1024
FF_TILES = FF_CHUNK // P
N_FF = D_FF // FF_CHUNK
MASKED = -1.0e30

C_Q, C_V, C_MQK, C_MV, C_MO = 0, 2048, 3072, 4096, 5120
C_IF, C_GATES = 6144, 6152

G_CKV, G_QK, G_V, G_GATE, G_MO, G_MQK, G_MV = 0, 8, 24, 32, 64, 72, 80
G_ABR, G_MBR, G_OUT, G_CQ, G_CO, G_FF = 88, 96, 104, 120, 124, 128
B_CKV, B_QK, B_V, B_GATE, B_MO, B_MQK, B_MV = 0, 2, 6, 8, 16, 18, 20
B_ABR, B_MBR, B_OUT, B_CQ, B_CROSS, B_CO, B_FF = 22, 26, 30, 34, 35, 36, 40
FF_GR = 2 * 4 + 4 * 2
FF_BLK = 6


def uses_before(blk, m):
    return blk - (1 if m >= 2 and blk >= 2 else 0)


def fulls_before(blk):
    if blk < 2:
        return 3 * blk
    return 3 * (blk - (1 if blk > B_CROSS else 0)) - 2


class Steps:

    def __init__(self, eng, sem):
        self.eng, self.sem, self.n, self.turn = eng, sem, 0, 0

    def __call__(self, ins):
        self.n += 1
        ins.then_inc(self.sem, 1)
        self.eng.wait_ge(self.sem, self.turn + self.n)


def hybrid_layer(nc, x, mem, norm_mix, w_in, b_igate, b_fgate, conv_w, conv_b, lam_q1, lam_k1, lam_q2, lam_k2,
                 attn_norm, mlstm_norm, w_attn_br, w_mlstm_br, w_out, norm_cross, norm_mem, w_cq, w_ckv, w_co,
                 norm_mlp, w_up, w_down, norm_final, out):
    ds = bass.ds
    KB = 1024
    NG = NT * MH

    def at(name, offset, shape, dt=F32):
        return nc.alloc_sbuf_tensor_at(name, shape, dt, offset=int(offset))

    cursor = [(nc.sbuf_base + 63) // 64 * 64]

    def const(name, shape, dt=F32):
        a = at(name, cursor[0], shape, dt)
        cursor[0] += (int(np.prod(shape[1:])) * 4 + 31) // 32 * 32
        return a

    ident = const("ident", [P, P])
    tri = const("tri", [P, P])
    ones = const("ones", [P, P])
    above = const("above", [P, P])
    alibi = const("alibi", [P, SEQ])
    vec = const("vec", [P, P])
    wif_raw = const("wif_raw", [P, KD, 2 * MH])
    wif_hi = const("wif_hi", [P, KD, 2 * MH], F32R)
    wif_lo = const("wif_lo", [P, KD, 2 * MH], F32R)
    bif = const("bif", [P, 2 * MH])
    lam_s = const("lam_s", [1, 4])
    neg_lam = const("neg_lam", [P, 1])
    turn_mark = const("turn_mark", [P, 1])
    eps_att = const("eps_att", [P, 1])
    eps_ml = const("eps_ml", [P, 1])
    half_neg = const("half_neg", [P, 8])
    gain_att = const("gain_att", [P, 1])
    ss_mem, var_mem, rs_mem = (const(f"{n}_mem", [P, MT]) for n in ("ss", "var", "rs"))
    ss_x, var_x, rs_x = (const(f"{n}_x", [P, NT]) for n in ("ss", "var", "rs"))
    neg_max, prob_sum, prob_inv, prob_max = (const(n, [P, 2]) for n in ("neg_max", "prob_sum", "prob_inv", "prob_max"))
    prob_scale = const("prob_scale", [P, 1])
    o_ms, o_var, o_rs = (const(n, [P, 1]) for n in ("o_ms", "o_var", "o_rs"))
    gif = const("gif", [P, NT, 2 * MH])
    gate_col = {n: const(f"g_{n}", [P, NG]) for n in
                ("logf", "neg_f", "abs_f", "exp_f", "ln_f", "b", "total", "u", "m_prev", "m_last", "m", "neg_m", "u_max")}
    pack = const("pack", [P, 4, NG])
    weight = const("weight", [P, 4, NG])
    den = const("den", [P, 4])
    h_ms, h_var, h_rs = (const(n, [P, 1]) for n in ("h_ms", "h_var", "h_rs"))
    x_sums = const("x_sums", [P, NT, 4])
    c_sum, c_var, c_rs, c_scale, c_neg, m_sum, m_var, m_inv, f_sum, f_var, f_rs = (
        const(n, [P, NT]) for n in ("c_sum", "c_var", "c_rs", "c_scale", "c_neg", "m_sum", "m_var", "m_inv",
                                    "f_sum", "f_var", "f_rs"))
    c_max, c_nm, c_den, c_inv = (const(n, [P, NT]) for n in ("c_max", "c_nm", "c_den", "c_inv"))
    RAW = cursor[0]

    V_MIX, V_MEM, V_CROSS, V_MLP, V_TAP, V_CB, V_ATT, V_ML, N_VEC = 0, 16, 32, 48, 64, 96, 104, 105, 113

    raw = [at(f"raw{s}", RAW + s * 8 * KB, [P, GR, BLK]) for s in range(4)]
    whi = [at(f"whi{s}", RAW + (32 + 8 * s) * KB, [P, GR, BLK], F32R) for s in range(2)]
    wlo = [at(f"wlo{s}", RAW + (48 + 8 * s) * KB, [P, GR, BLK], F32R) for s in range(2)]

    A = RAW + 64 * KB
    act_hi = at("act_hi", A, [P, KD, SEQ], F32R)
    act_lo = at("act_lo", A + 32 * KB, [P, KD, SEQ], F32R)
    x_junk = [at(f"x_junk{t}", A + t * 8 * KB, [P, D]) for t in range(NT)]
    mem_junk = [at(f"mem_junk{t}", A + (32 + t * 8) * KB, [P, D]) for t in range(MT)]
    vec_rows = at("vec_rows", A + 48 * KB, [P, P])
    lam_in = at("lam_in", A + 49 * KB, [1, 4, QK])
    lam_pr = at("lam_pr", A + 50 * KB, [1, 2, QK])
    hmT = at("hmT", A, [P, KD // 2, SEQ])
    moT = at("moT", A + 16 * KB, [P, KD // 2, SEQ])
    y1T = at("y1T", A + 32 * KB, [P, KD, SEQ])

    R = A + 64 * KB
    memT_hi = at("memT_hi", R, [P, KD, MEM], F32R)
    memT_lo = at("memT_lo", R + 16 * KB, [P, KD, MEM], F32R)
    akT = at("akT", R, [P, HEADS, SEQ])
    av = at("av", R + 16 * KB, [P, NT, HEADS * P])
    br_hi = at("br_hi", R, [P, FF_TILES, SEQ], F32R)
    br_lo = at("br_lo", R + 16 * KB, [P, FF_TILES, SEQ], F32R)
    coT_hi = at("coT_hi", R, [P, CH, SEQ], F32R)
    coT_lo = at("coT_lo", R + 8 * KB, [P, CH, SEQ], F32R)
    cprob = [at(f"cprob{b}", R + (16 + 4 * b) * KB, [P, NT, MEM]) for b in range(2)]
    R2 = R + 32 * KB
    xs = at("xs", R2, [P, NT, D])
    aqT = at("aqT", R2, [P, HEADS, SEQ])
    vaug = at("vaug", R2, [P, NT, MH, MV + 1])
    score = [at(f"score{b}", R2 + (16 + 4 * b) * KB, [P, 2, SEQ]) for b in range(2)]
    wmix = at("wmix", R2 + 24 * KB, [P, SEQ])
    wmixT = at("wmixT", R2 + 26 * KB, [P, SEQ])
    qh = at("qh", R2 + 28 * KB, [P, SEQ])
    o_sb = at("o_sb", R2 + 30 * KB, [P, P])
    uT = at("uT", R2 + 16 * KB, [NG, P])
    cmT = at("cmT", R2 + 17 * KB, [NG, P])
    diag_cm = at("diag_cm", R2 + 18 * KB, [NG, NG])
    mqkT = at("mqkT", R2 + 16 * KB + 256, [P, 2 * MH, SEQ])
    S = R2 + 32 * KB + 256
    mem_sb = at("mem_sb", S + 4 * KB, [P, MT, D])
    junk = at("junk", S, [P, SEQ])
    gate_out = at("gate_out", S + 2 * KB, [P, 4, SEQ])
    kh = at("kh", S + 10 * KB, [P, SEQ])
    sig_e = [at(f"sig_e{b}", S + (2 + 2 * b) * KB, [P, SEQ]) for b in range(2)]
    gate_in = [at(f"gate_in{b}", S + 2 * b * KB, [P, SEQ]) for b in range(2)]
    M0 = S + 4 * KB
    ew = at("ew", M0, [P, P])
    kw = at("kw", M0 + 512, [P, P])
    diag = at("diag", M0 + 1024, [P, P])
    inter = at("inter", M0 + 1536, [P, MV + 1])
    num = at("num", M0 + 2592, [P, MV + 1])
    state = at("state", M0 + 3648, [P, MH, MV + 1])
    ysum = [at(f"ysum{b}", M0 + 2 * b * KB, [P, SEQ]) for b in range(2)]
    cqT = at("cqT", S + 2 * KB, [P, CH, SEQ])
    probT = [at("probT0", S + 10 * KB, [P, SEQ]), at("probT1", R + 24 * KB, [P, SEQ])]
    relu_t = [at(f"relu_t{b}", S + (2 + 2 * b) * KB, [P, SEQ]) for b in range(2)]
    sq_t = [at(f"sq_t{b}", S + (6 + 2 * b) * KB, [P, SEQ]) for b in range(2)]
    CK = S + 13 * KB
    ckT = at("ckT", CK, [P, CH, MEM])
    cv = at("cv", CK + 4 * KB, [P, MT, CH * P])
    gain_f = at("gain_f", S + 10 * KB, [P, D])
    assert 3648 + MH * (MV + 1) * 4 <= 9 * KB

    acc = [nc.alloc_psum_tensor(f"acc{m}", [P, BLK], F32) for m in range(4)]
    aux = [nc.alloc_psum_tensor(f"aux{m}", [P, BLK], F32) for m in range(4)]

    gates_dram = nc.dram_tensor("gates_scratch", [10, P, 4 * SEQ], F32).ap()

    sem = nc.alloc_semaphore
    vec_loaded, lam_loaded, if_loaded, fin_loaded, mo_loaded, x_again = (
        sem(n) for n in ("vec_loaded", "lam_loaded", "if_loaded", "fin_loaded", "mo_loaded", "x_again"))
    x_loaded = [sem(f"x_loaded{t}") for t in range(NT)]
    m_loaded = [sem(f"m_loaded{t}") for t in range(MT)]
    raw_loaded = [sem(f"raw_loaded{s}") for s in range(4)]
    gate_loaded = [sem(f"gate_loaded{b}") for b in range(2)]
    gate_stored, out_stored = sem("gate_stored"), sem("out_stored")
    hi_ready, lo_ready, granule_used, bank_full = (sem(n) for n in ("hi_ready", "lo_ready", "granule_used", "bank_full"))
    bank_free = [sem(f"bank_free{m}") for m in range(4)]
    dve_step, act_step, pool_step = sem("dve_step"), sem("act_step"), sem("pool_step")
    pool_const, vec_full, vec_ready, mem_ss, mem_rs, mem_scaled, memT_full, memT_hi_ok, memT_lo_ok = (
        sem(n) for n in ("pool_const", "vec_full", "vec_ready", "mem_ss", "mem_rs", "mem_scaled", "memT_full",
                         "memT_hi_ok", "memT_lo_ok"))
    x_ss, x_rs, x_scaled, xT_full, xT_hi_ok, xT_lo_ok = (
        sem(n) for n in ("x_ss", "x_rs", "x_scaled", "xT_full", "xT_hi_ok", "xT_lo_ok"))
    lam_dots, lam_exp, lam_val, lam_full = (sem(n) for n in ("lam_dots", "lam_exp", "lam_val", "lam_full"))
    qh_ready, scores_full, max_ready, probs_ready, mix_ready, mixT_full, mixT_ready = (
        sem(n) for n in ("qh_ready", "scores_full", "max_ready", "probs_ready", "mix_ready", "mixT_full", "mixT_ready"))
    att_full, att_ms, att_rs, att_scaled, attT_full, att_hi, att_lo = (
        sem(n) for n in ("att_full", "att_ms", "att_rs", "att_scaled", "attT_full", "att_hi", "att_lo"))
    wif_hi_ok, wif_lo_ok, if_full, abs_ready, soft_ready, logf_ready, cum_full, u_ready, uT_full, cm_ready, cm_full = (
        sem(n) for n in ("wif_hi_ok", "wif_lo_ok", "if_full", "abs_ready", "soft_ready", "logf_ready", "cum_full",
                         "u_ready", "uT_full", "cm_ready", "cm_full"))
    pack_ready, weight_ready, conv_first, silu_exp, mqk_ready, state_zero = (
        sem(n) for n in ("pack_ready", "weight_ready", "conv_first", "silu_exp", "mqk_ready", "state_zero"))
    diag_ready, dqk_full, e_ready, w_ready, n_full, c_full, c_ready = (
        sem(n) for n in ("diag_ready", "dqk_full", "e_ready", "w_ready", "n_full", "c_full", "c_ready"))
    inter_ready, den_ready, h_sq, h_rs_ok, h_ready, hT_full, hm_ready, hm_hi, hm_lo = (
        sem(n) for n in ("inter_ready", "den_ready", "h_sq", "h_rs_ok", "h_ready", "hT_full", "hm_ready", "hm_hi", "hm_lo"))
    ys_ready, y_hi, y_lo, x1_sq, c_stat, c_rs_ok, x1T_full, x1T_hi, x1T_lo = (
        sem(n) for n in ("ys_ready", "y_hi", "y_lo", "x1_sq", "c_stat", "c_rs_ok", "x1T_full", "x1T_hi", "x1T_lo"))
    cs_full, cmax_ready, cexp_ready, cprob_ready, cT_full, cT_act, cT_dve, co_full, co_hi, co_lo = (
        sem(n) for n in ("cs_full", "cmax_ready", "cexp_ready", "cprob_ready", "cT_full", "cT_act", "cT_dve",
                         "co_full", "co_hi", "co_lo"))
    x2_sq, x2T_full, x2T_hi, x2T_lo, relu_ready, hid_hi, hid_lo, x3_sq, f_stat, f_rs_ok, out_ready = (
        sem(n) for n in ("x2_sq", "x2T_full", "x2T_hi", "x2T_lo", "relu_ready", "hid_hi", "hid_lo", "x3_sq",
                         "f_stat", "f_rs_ok", "out_ready"))

    def wait_bank(eng, blk, m, n_last, turn=0, per=4, last_bank=3):
        if m < last_bank:
            eng.wait_ge(bank_full, turn * 3 + (fulls_before(blk) + m + 1))
        else:
            eng.wait_ge(granule_used, turn * per + (n_last + 1))

    def freed(blk, m, turn=0):
        return turn + (uses_before(blk, m) + 1)

    x_v = x[0].rearrange("(t p) d -> p t d", p=P)
    mem_v = mem[0].rearrange("(t p) d -> p t d", p=P)
    out_v = out[0].rearrange("(t p) d -> p t d", p=P)

    def rows(w):
        return w[0].rearrange("(k p) n -> p k n", p=P)

    w_in_v, w_abr_v, w_mbr_v, w_out_v = rows(w_in), rows(w_attn_br), rows(w_mlstm_br), rows(w_out)
    w_cq_v, w_ckv_v, w_co_v, w_up_v, w_down_v = rows(w_cq), rows(w_ckv), rows(w_co), rows(w_up), rows(w_down)

    def cols(k, n=P):
        return slice(k * n, (k + 1) * n)

    ctx = ExitStack()
    block = ctx.enter_context(nc.Block())

    @block.sync
    def _(sp):
        def load(n, slot, src, turn=0, per=0):
            if n >= 4:
                sp.wait_ge(lo_ready, turn * per + (n - 3))
            sp.dma_start(raw[slot][:], src).then_inc(raw_loaded[slot], 16)

        for first, count, src in ((V_MIX, 16, norm_mix), (V_MEM, 16, norm_mem), (V_CROSS, 16, norm_cross),
                                  (V_MLP, 16, norm_mlp), (V_CB, 8, conv_b), (V_ATT, 1, attn_norm), (V_ML, 8, mlstm_norm)):
            sp.dma_start(vec_rows[first:first + count, :], src.rearrange("a (k p) -> (a k) p", p=P)).then_inc(vec_loaded, 16)
        sp.dma_start(vec_rows[V_TAP:V_TAP + 32, :], conv_w[0].rearrange("w (k p) -> (w k) p", p=P)).then_inc(vec_loaded, 16)
        for t in range(MT):
            sp.dma_start(mem_sb[:, t, :], mem_v[:, t, :]).then_inc(m_loaded[t], 16)
        for g in range(2):
            load(G_CKV + g, g, w_ckv_v[:, GR * g:GR * g + GR, 0:BLK])
        for t in range(NT):
            sp.dma_start(xs[:, t, :], x_v[:, t, :]).then_inc(x_loaded[t], 16)
        for g in range(2, 4):
            load(G_CKV + g, g, w_ckv_v[:, GR * g:GR * g + GR, 0:BLK])
        for k, v in enumerate((lam_q1, lam_k1, lam_q2, lam_k2)):
            sp.dma_start(lam_in[0:1, k, :], v).then_inc(lam_loaded, 16)
        sp.dma_start(wif_raw[:], w_in_v[:, :, C_IF:C_IF + 2 * MH]).then_inc(if_loaded, 16)
        sp.dma_start(bif[:, 0:MH], b_igate[0].partition_broadcast(P)).then_inc(if_loaded, 16)
        sp.dma_start(bif[:, MH:2 * MH], b_fgate[0].partition_broadcast(P)).then_inc(if_loaded, 16)
        for g in range(4):
            load(G_CKV + 4 + g, g, w_ckv_v[:, GR * g:GR * g + GR, BLK:2 * BLK])

        def wide_blocks(w, first_granule, first_column, first, blocks):
            with sp.Fori(first, blocks) as i:
                for g in range(4):
                    load(first_granule + g, g, w[:, GR * g:GR * g + GR, ds(i * BLK + first_column, BLK)], turn=i, per=4)

        wide_blocks(w_in_v, G_QK, C_Q, 0, 4)
        wide_blocks(w_in_v, G_V, C_V, 0, 2)
        wide_blocks(w_in_v, G_GATE, C_GATES, 0, 8)
        wide_blocks(w_in_v, G_MO, C_MO, 0, 2)
        wide_blocks(w_in_v, G_MQK, C_MQK, 0, 2)
        wide_blocks(w_in_v, G_MV, C_MV, 0, 2)

        def gate_tile(k):
            if 2 <= k < KD + 2:
                sp.wait_ge(bank_free[(k - 2) % 4], freed(B_ABR + (k - 2) // 4, (k - 2) % 4))
            elif k >= KD + 2:
                sp.wait_ge(ys_ready, k - 1 - KD)
            sp.dma_start(gate_in[k % 2][:], gates_dram[k // 4, :, cols(k % 4, SEQ)]).then_inc(gate_loaded[k % 2], 16)

        for g in range(2):
            load(G_ABR + g, g, w_abr_v[:, GR * g:GR * g + GR, 0:BLK])
        sp.wait_ge(gate_stored, 10 * 16)
        sp.wait_ge(granule_used, G_ABR)
        sp.dma_start(moT[:].rearrange("p (a k) t -> p a (k t)", a=2),
                     gates_dram[8:10].rearrange("a p n -> p a n")).then_inc(mo_loaded, 16)
        gate_tile(0)
        gate_tile(1)
        for j in range(1, 8):
            w, jj = (w_abr_v, j) if j < 4 else (w_mbr_v, j - 4)
            for g in range(2):
                load(G_ABR + 2 * j + g, (2 * j + g) % 4, w[:, GR * g:GR * g + GR, cols(jj, BLK)])
            if j == 5:
                sp.wait_ge(hm_lo, KD // 2)
                sp.dma_start(xs[:], x_v).then_inc(x_again, 16)
            for m in range(4):
                gate_tile(4 * (j - 1) + m + 2)
        for g in range(2):
            load(G_OUT + g, g, w_out_v[:, GR * g:GR * g + GR, 0:BLK])
        gate_tile(30)
        gate_tile(31)
        for g in range(2, 4):
            load(G_OUT + g, g, w_out_v[:, GR * g:GR * g + GR, 0:BLK])
        wide_blocks(w_out_v, G_OUT, 0, 1, 4)
        for g in range(4):
            load(G_CQ + g, g, w_cq_v[:, GR * g:GR * g + GR, :])
        for j in range(4):
            load(G_CO + j, j, w_co_v[:, :, cols(j, BLK)])
        with sp.Fori(0, N_FF) as i:
            for j in range(2):
                for g in range(4):
                    load(G_FF + 4 * j + g, g, w_up_v[:, GR * g:GR * g + GR, ds(i * FF_CHUNK + BLK * j, BLK)],
                         turn=i, per=FF_GR)
            for j in range(4):
                for g in range(2):
                    load(G_FF + 8 + 2 * j + g, (2 * j + g) % 4,
                         w_down_v[:, ds(i * FF_TILES + GR * g, GR), cols(j, BLK)], turn=i, per=FF_GR)
        sp.dma_start(gain_f[:], norm_final.partition_broadcast(P)).then_inc(fin_loaded, 16)
        for t in range(NT):
            sp.wait_ge(out_ready, t + 1)
            sp.dma_start(out_v[:, t, :], xs[:, t, :]).then_inc(out_stored, 16)
        sp.wait_ge(out_stored, NT * 16)

    @block.gpsimd
    def _(pool):
        step = Steps(pool, pool_step)
        step(nc.gpsimd.memset(ident[:], 0.0))
        nc.gpsimd.affine_select(out=ident[:], in_=ident[:], compare_op=ALU.not_equal, fill=1.0, base=0,
                                pattern=[[-1, P]], channel_multiplier=1).then_inc(pool_const, 1)
        nc.gpsimd.memset(eps_att[:], P * EPS)
        nc.gpsimd.memset(eps_ml[:], MV * EPS)
        step(nc.gpsimd.memset(half_neg[:], -0.5))
        nc.gpsimd.memset(ones[:], 1.0).then_inc(pool_const, 1)
        step(nc.gpsimd.memset(tri[:], 1.0))
        nc.gpsimd.affine_select(out=tri[:], in_=tri[:], compare_op=ALU.is_ge, fill=0.0, base=0,
                                pattern=[[1, P]], channel_multiplier=-1).then_inc(pool_const, 1)
        step(nc.gpsimd.memset(above[:], 0.0))
        nc.gpsimd.affine_select(out=above[:], in_=above[:], compare_op=ALU.is_ge, fill=MASKED, base=0,
                                pattern=[[1, P]], channel_multiplier=-1).then_inc(pool_const, 1)
        inv = int(QK ** 0.5)
        step(nc.gpsimd.iota(alibi[:], pattern=[[inv, SEQ]], base=-inv * (SEQ - P), channel_multiplier=-inv,
                            allow_small_or_imprecise_dtypes=True))
        nc.gpsimd.affine_select(out=alibi[:], in_=alibi[:], compare_op=ALU.is_ge, fill=MASKED, base=SEQ - P,
                                pattern=[[-1, SEQ]], channel_multiplier=1).then_inc(pool_const, 1)

        def inv_rms(out_ap, var, sums, width, done):
            step(nc.gpsimd.tensor_scalar(var, sums, 1.0 / width, EPS, ALU.mult, ALU.add))
            nc.gpsimd.tensor_tensor(out_ap, var, half_neg[:, 0:var.shape[1]], ALU.pow).then_inc(done, 1)

        for t in range(MT):
            pool.wait_ge(mem_ss, t + 1)
            inv_rms(rs_mem[:, t:t + 1], var_mem[:, t:t + 1], ss_mem[:, t:t + 1], D, mem_rs)
        for t in range(NT):
            pool.wait_ge(x_ss, t + 1)
            inv_rms(rs_x[:, t:t + 1], var_x[:, t:t + 1], ss_x[:, t:t + 1], D, x_rs)

        def inv_rms_loop(turns, sums, eps, var, out_ap, ready, done):
            base = step.n
            with pool.Fori(0, turns) as i:
                step.turn = i
                pool.wait_ge(ready, i + 1)
                step(nc.gpsimd.tensor_tensor(var[:], sums[:], eps[:], ALU.add))
                nc.gpsimd.tensor_tensor(out_ap[:], var[:], half_neg[:, 0:1], ALU.pow).then_inc(done, 1)
            step.turn, step.n = 0, base + turns

        inv_rms_loop(HEADS * NT, o_ms, eps_att, o_var, o_rs, att_ms, att_rs)
        inv_rms_loop(NG, h_ms, eps_ml, h_var, h_rs, h_sq, h_rs_ok)
        pool.wait_ge(c_stat, 1)
        inv_rms(c_rs[:], c_var[:], c_sum[:], D, c_rs_ok)
        pool.wait_ge(f_stat, 1)
        inv_rms(f_rs[:], f_var[:], f_sum[:], D, f_rs_ok)

    @block.scalar
    def _(act):
        step = Steps(act, act_step)

        def split(n, turn=0, per=0):
            act.wait_ge(raw_loaded[n % 4], turn * (per * 4) + (n // 4 + 1) * 16)
            if n >= 2:
                act.wait_ge(granule_used, turn * per + (n - 1))
            nc.scalar.activation(whi[n % 2][:], raw[n % 4][:], ACT.Copy).then_inc(hi_ready, 1)

        def evac(blk, m, n_last, dst, src, turn=0, last_bank=3):
            wait_bank(act, blk, m, n_last, turn, last_bank=last_bank)
            nc.scalar.activation(dst, src, ACT.Copy).then_inc(bank_free[m], 1)

        def transposed_hi(k, full, bank, dst, gain, done):
            act.wait_ge(full, k + 1)
            nc.scalar.activation(dst, bank, ACT.Identity, scale=vec[:, gain + k:gain + k + 1]).then_inc(done, 1)

        for t in range(MT):
            act.wait_ge(m_loaded[t], 16)
            nc.scalar.activation(mem_junk[t][:], mem_sb[:, t, :], ACT.Square, accum_out=ss_mem[:, t:t + 1]).then_inc(mem_ss, 1)
        act.wait_ge(vec_ready, 1)
        for k in range(KD):
            transposed_hi(k, memT_full, aux[k % 4][:, 0:MEM], memT_hi[:, k, :], V_MEM, memT_hi_ok)
        split(G_CKV)
        for g in range(4):
            act.wait_ge(x_loaded[g], 16)
            nc.scalar.activation(x_junk[g][:], xs[:, g, :], ACT.Square, accum_out=ss_x[:, g:g + 1]).then_inc(x_ss, 1)
            split(G_CKV + g + 1)
        act.wait_ge(lam_dots, 1)
        nc.scalar.activation(lam_s[0:1, 2:4], lam_s[0:1, 0:2], ACT.Exp).then_inc(lam_exp, 1)
        for m in range(4):
            evac(B_CKV, m, G_CKV + 3, ckT[:, m, :], acc[m][:, 0:MEM])
        for g in range(4):
            for k in range(4 * g, 4 * g + 4):
                transposed_hi(k, xT_full, aux[k % 4][:], act_hi[:, k, :], V_MIX, xT_hi_ok)
            split(G_CKV + 5 + g)
        for m in range(MT):
            evac(B_CKV + 1, m, G_CKV + 7, cv[:, m, :], acc[m][:], last_bank=1)

        def plain_blocks(blk, n, count, dst):
            with act.Fori(0, count) as i:
                for g in range(4):
                    split(n + g + 1, i, 4)
                for m in range(4):
                    evac(blk, m, n + 3, dst(i, m), acc[m][:], turn=i)

        plain_blocks(B_QK, G_QK, 2, lambda i, m: aqT[:, ds(i * 4 + m, 1), :])
        plain_blocks(B_QK + 2, G_QK + 8, 2, lambda i, m: akT[:, ds(i * 4 + m, 1), :])
        plain_blocks(B_V, G_V, 2, lambda i, m: av[:, m, ds(i * BLK, BLK)])

        def gate_evac(blk, m, n_last, turn):
            wait_bank(act, blk, m, n_last, turn)
            nc.scalar.activation(gate_out[:, m, :], acc[m][:], ACT.Tanh, scale=0.5).then_inc(bank_free[m], 1)

        def gate_store(blk, turn, first):
            act.wait_ge(bank_free[3], freed(blk, 3, turn))
            act.dma_start(gates_dram[ds(turn + first, 1)].rearrange("a p n -> p (a n)"),
                          gate_out[:].rearrange("p k t -> p (k t)")).then_inc(gate_stored, 16)

        def attention_head(h, first):
            for g in range(NT):
                n, done = (g + 1) * P, h * NT + (g + 1)
                act.wait_ge(max_ready, done)
                for mp in range(2):
                    ins = nc.scalar.activation(score[g % 2][:, mp, 0:n], score[g % 2][:, mp, 0:n], ACT.Exp,
                                               bias=neg_max[:, mp:mp + 1], scale=QK ** -0.5,
                                               accum_out=prob_sum[:, mp:mp + 1])
                ins.then_inc(probs_ready, 1)
                split(G_GATE + g + 1, h, 4)
                if g == 3:
                    if not first:
                        act.wait_ge(gate_stored, h * 16)
                    gate_evac(B_GATE, 0, G_GATE + 3, h)
                act.wait_ge(mixT_full, done)
                nc.scalar.activation(wmixT[:, 0:n], aux[2][:, 0:n], ACT.Copy).then_inc(mixT_ready, 1)
                if g == 3:
                    gate_evac(B_GATE, 1, G_GATE + 3, h)
                act.wait_ge(att_full, done)
                nc.scalar.activation(junk[:, 0:P], aux[3][:, 0:P], ACT.Square, accum_out=o_ms[:]).then_inc(att_ms, 1)
                if g == 3:
                    gate_evac(B_GATE, 2, G_GATE + 3, h)
                    gate_evac(B_GATE, 3, G_GATE + 3, h)
                    gate_store(B_GATE, h, 0)

        attention_head(0, True)
        with act.Fori(1, HEADS) as h:
            attention_head(h, False)

        act.wait_ge(if_loaded, 48)
        nc.scalar.activation(wif_hi[:], wif_raw[:], ACT.Copy).then_inc(wif_hi_ok, 1)
        for j in range(2):
            for g in range(4):
                if (j, g) == (0, 0):
                    act.wait_ge(abs_ready, 1)
                    step(nc.scalar.activation(gate_col["exp_f"][:], gate_col["abs_f"][:], ACT.Exp, scale=-1.0))
                    nc.scalar.activation(gate_col["ln_f"][:], gate_col["exp_f"][:], ACT.Ln, bias=1.0).then_inc(soft_ready, 1)
                split(G_MO + 4 * j + g + 1)
                if j == 1:
                    for k in (2 * g, 2 * g + 1):
                        nc.scalar.activation(br_hi[:, k, :], aqT[:, k, :], ACT.Copy).then_inc(att_hi, 1)
            if j == 0:
                act.wait_ge(pack_ready, 1)
                nc.scalar.activation(weight[:], pack[:], ACT.Exp).then_inc(weight_ready, 1)
            act.wait_ge(gate_stored, (8 + j) * 16)
            for m in range(4):
                gate_evac(B_MO + j, m, G_MO + 4 * j + 3, 0)
            gate_store(B_MO + j, 0, 8 + j)

        def silu_exponential(k):
            act.wait_ge(bank_free[k % 4], freed(B_MQK + k // 4, k % 4))
            if k >= 2:
                act.wait_ge(mqk_ready, k - 1)
            nc.scalar.activation(sig_e[k % 2][:], mqkT[:, k, :], ACT.Exp, scale=-1.0).then_inc(silu_exp, 1)

        act.wait_ge(gate_stored, 10 * 16)
        for j in range(2):
            for g in range(4):
                split(G_MQK + 4 * j + g + 1)
                if j == 1:
                    silu_exponential(g)
            for m in range(4):
                k = 4 * j + m
                wait_bank(act, B_MQK + j, m, G_MQK + 4 * j + 3)
                nc.scalar.activation(mqkT[:, k, :], acc[m][:], ACT.Identity, scale=vec[:, V_TAP + 24 + k:V_TAP + 25 + k],
                                     bias=vec[:, V_CB + k:V_CB + k + 1]).then_inc(conv_first, 1)
        act.wait_ge(att_lo, HEADS)
        for j in range(2):
            for g in range(4):
                split(G_MV + 4 * j + g + 1)
                if j == 0:
                    silu_exponential(4 + g)
            for m in range(4):
                evac(B_MV + j, m, G_MV + 4 * j + 3, vaug[:, m, 2 * j:2 * j + 2, 0:MV],
                     acc[m][:].rearrange("p (h v) -> p h v", h=2))

        def unit_first(u):
            act.wait_ge(dqk_full, u + 1)
            nc.scalar.activation(ew[:], aux[0][:, 0:P], ACT.Exp, bias=gate_col["u"][:, u:u + 1]).then_inc(e_ready, 1)

        def unit_second(u):
            act.wait_ge(n_full, u + 1)
            nc.scalar.activation(inter[:], aux[1][:, 0:MV + 1], ACT.Identity, scale=weight[:, 0, u:u + 1]).then_inc(inter_ready, 1)
            act.wait_ge(den_ready, u + 1)
            nc.scalar.activation(inter[:, 0:MV], num[:, 0:MV], ACT.Square, scale=den[:, 2:3],
                                 accum_out=h_ms[:]).then_inc(h_sq, 1)

        for g in range(8):
            unit_first(2 * g)
            split(G_ABR + g + 1)
            unit_second(2 * g)
            unit_first(2 * g + 1)
            unit_second(2 * g + 1)

        act.wait_ge(hm_ready, 2 * NG)
        for k in range(KD // 2):
            nc.scalar.activation(br_hi[:, k, :], hmT[:, k, :], ACT.Copy).then_inc(hm_hi, 1)
        for j in range(4):
            for g in range(2):
                split(G_MBR + 2 * j + g + 1)
            for k in range(4 * j, 4 * j + 4):
                act.wait_ge(ys_ready, k + 1)
                nc.scalar.activation(act_hi[:, k, :], ysum[k % 2][:], ACT.Copy).then_inc(y_hi, 1)

        def squares(blk, m, j, done, before, turn=0):
            act.wait_ge(bank_free[m], freed(blk, m, turn))
            if before is not None:
                act.wait_ge(done, before)
            nc.scalar.activation(junk[:], xs[:, m, cols(j, BLK)], ACT.Square, accum_out=x_sums[:, m, j:j + 1]).then_inc(done, 1)

        for j in range(4):
            for g in range(4):
                split(G_OUT + 4 * j + g + 1)
            for m in range(4):
                squares(B_OUT + j, m, j, x1_sq, 4 * j + m or None)
        for g in range(4):
            for k in range(4 * g, 4 * g + 4):
                transposed_hi(k, x1T_full, aux[k % 4][:], act_hi[:, k, :], V_CROSS, x1T_hi)
            split(G_CQ + g + 1)
        for m in range(4):
            evac(B_CQ, m, G_CQ + 3, cqT[:, m, :], acc[m][:])

        def cross_exponentials(h):
            act.wait_ge(cmax_ready, h + 1)
            for t in range(NT):
                nc.scalar.activation(cprob[h % 2][:, t, :], aux[t // 2][:, cols(t % 2, MEM)], ACT.Exp,
                                     bias=c_nm[:, t:t + 1], scale=c_scale[:, t:t + 1],
                                     accum_out=c_den[:, t:t + 1]).then_inc(cexp_ready, 1)

        cross_exponentials(0)
        for h in range(CH):
            act.wait_ge(cT_full, 2 * h + 1)
            nc.scalar.activation(probT[0][:], aux[2][:], ACT.Copy).then_inc(cT_act, 1)
            if h + 1 < CH:
                cross_exponentials(h + 1)
            act.wait_ge(co_full, h + 1)
            nc.scalar.activation(coT_hi[:, h, :], acc[h][:], ACT.Copy).then_inc(co_hi, 1)

        def mlp_input_hi(j):
            for k in range(4 * j, 4 * j + 4):
                transposed_hi(k, x2T_full, aux[k % 4][:], act_hi[:, k, :], V_MLP, x2T_hi)

        for j in range(4):
            split(G_CO + j + 1)
            if j:
                mlp_input_hi(j - 1)
            for m in range(4):
                squares(B_CO + j, m, j, x2_sq, 4 * j + m or None)
        mlp_input_hi(3)

        def hidden_hi(i, k):
            act.wait_ge(bank_free[k % 4], freed(B_FF + k // 4, k % 4, i * FF_BLK))
            nc.scalar.activation(br_hi[:, k, :], sq_t[k % 2][:], ACT.Copy).then_inc(hid_hi, 1)

        def ff_chunk(i, first=False, last=False):
            for j in range(2):
                for g in range(4):
                    split(G_FF + 4 * j + g + 1, i, FF_GR)
                for k in range(4 * j, 4 * j + 4):
                    wait_bank(act, B_FF + j, k % 4, G_FF + 4 * j + 3, i * FF_BLK) if k % 4 < 3 else \
                        act.wait_ge(granule_used, i * FF_GR + (G_FF + 4 * j + 4))
                    nc.scalar.activation(relu_t[k % 2][:], acc[k % 4][:], ACT.Relu).then_inc(relu_ready, 1)
                    if k % 4:
                        hidden_hi(i, k - 1)
                hidden_hi(i, 4 * j + 3)
            for j in range(4):
                for g in range(2):
                    if not (last and (j, g) == (3, 1)):
                        split(G_FF + 8 + 2 * j + g + 1, i, FF_GR)
                for m in range(4):
                    k = 4 * j + m
                    squares(B_FF + 2 + j, m, j, x3_sq, None if first and k == 0 else i * 16 + k, i * FF_BLK)

        ff_chunk(0, first=True)
        with act.Fori(1, N_FF - 1) as i:
            ff_chunk(i)
        ff_chunk(N_FF - 1, last=True)

    @block.vector
    def _(dve):
        step = Steps(dve, dve_step)

        def split(n, turn=0, per=0):
            dve.wait_ge(hi_ready, turn * per + (n + 1))
            nc.vector.tensor_tensor(wlo[n % 2][:], raw[n % 4][:], whi[n % 2][:].bitcast(F32), ALU.subtract).then_inc(lo_ready, 1)

        def transposed_lo(k, hi_ok, bank, dst, hi, gain, done):
            dve.wait_ge(hi_ok, k + 1)
            nc.vector.scalar_tensor_tensor(out=dst, in0=bank, scalar=vec[:, gain + k:gain + k + 1], in1=hi.bitcast(F32),
                                           op0=ALU.mult, op1=ALU.subtract).then_inc(done, 1)

        dve.wait_ge(vec_full, 1)
        nc.vector.tensor_copy(vec[:, 0:N_VEC], aux[3][:, 0:N_VEC]).then_inc(vec_ready, 1)
        dve.wait_ge(vec_ready, 1)
        nc.vector.tensor_scalar(gain_att[:], vec[:, V_ATT:V_ATT + 1], 1.0 - LAM_INIT, None, ALU.mult)
        for t in range(MT):
            dve.wait_ge(mem_rs, t + 1)
            nc.vector.tensor_scalar(mem_sb[:, t, :], mem_sb[:, t, :], rs_mem[:, t:t + 1], None, ALU.mult).then_inc(mem_scaled, 1)
        for k in range(KD):
            transposed_lo(k, memT_hi_ok, aux[k % 4][:, 0:MEM], memT_lo[:, k, :], memT_hi[:, k, :], V_MEM, memT_lo_ok)
        split(G_CKV)
        dve.wait_ge(lam_loaded, 64)
        step(nc.vector.tensor_tensor(lam_pr[:], lam_in[0:1, 0:4:2, :], lam_in[0:1, 1:4:2, :], ALU.mult))
        nc.vector.reduce_sum(lam_s[0:1, 0:2], lam_pr[:], AX).then_inc(lam_dots, 1)
        for g in range(4):
            split(G_CKV + g + 1)
            dve.wait_ge(x_rs, g + 1)
            nc.vector.tensor_scalar(xs[:, g, :], xs[:, g, :], rs_x[:, g:g + 1], None, ALU.mult).then_inc(x_scaled, 1)
        dve.wait_ge(lam_exp, 1)
        step(nc.vector.tensor_tensor(lam_s[0:1, 0:1], lam_s[0:1, 3:4], lam_s[0:1, 2:3], ALU.subtract))
        nc.vector.tensor_scalar(lam_s[0:1, 1:2], lam_s[0:1, 0:1], -LAM_INIT, None, ALU.add).then_inc(lam_val, 1)
        for g in range(4):
            for k in range(4 * g, 4 * g + 4):
                transposed_lo(k, xT_hi_ok, aux[k % 4][:], act_lo[:, k, :], act_hi[:, k, :], V_MIX, xT_lo_ok)
            split(G_CKV + 5 + g)
        dve.wait_ge(lam_full, 1)
        nc.vector.tensor_copy(neg_lam[:], aux[0][:, 0:1])

        with dve.Fori(0, 6) as i:
            for g in range(4):
                split(G_QK + g + 1, i, 4)

        dve.wait_ge(pool_const, 5)
        base = step.n

        def attention_output(h, g):
            dve.wait_ge(att_rs, h * NT + (g + 1))
            nc.vector.tensor_scalar(o_sb[:], aux[3][:, 0:P], o_rs[:], P ** 0.5, ALU.mult, ALU.mult).then_inc(att_scaled, 1)

        def attention_transposed(h, g):
            dve.wait_ge(attT_full, h * NT + (g + 1))
            nc.vector.tensor_scalar(aqT[:, ds(h, 1), cols(g)].rearrange("p a t -> p (a t)"), aux[3][:, P:2 * P], gain_att[:],
                                    None, ALU.mult)

        steps_per_head = 1 + NT * 4
        with dve.Fori(0, HEADS) as h:
            step.turn = h * steps_per_head
            step(nc.vector.tensor_scalar(alibi[:], alibi[:], 0.5, None, ALU.mult))
            nc.vector.tensor_copy(kh[:], akT[:, ds(h, 1), :].rearrange("p a t -> p (a t)"))
            nc.vector.tensor_copy(qh[:], aqT[:, ds(h, 1), :].rearrange("p a t -> p (a t)")).then_inc(qh_ready, 1)
            for g in range(NT):
                n, done = (g + 1) * P, h * NT + (g + 1)
                dve.wait_ge(scores_full, done)
                nc.vector.memset(turn_mark[:], 0.0)
                nc.vector.tensor_tensor_reduce(out=score[g % 2][:, 0, 0:n], in0=aux[0][:, 0:n],
                                                in1=alibi[:, SEQ - n:SEQ], scale=1.0, scalar=-3.0e38, op0=ALU.add,
                                                op1=ALU.max, accum_out=prob_max[:, 0:1])
                step(nc.vector.tensor_tensor_reduce(out=score[g % 2][:, 1, 0:n], in0=aux[1][:, 0:n],
                                                    in1=alibi[:, SEQ - n:SEQ], scale=1.0, scalar=-3.0e38, op0=ALU.add,
                                                    op1=ALU.max, accum_out=prob_max[:, 1:2]))
                nc.vector.tensor_scalar(neg_max[:], prob_max[:], -(QK ** -0.5), None, ALU.mult).then_inc(max_ready, 1)
                if g == 1:
                    attention_transposed(h, 0)
                dve.wait_ge(probs_ready, done)
                step(nc.vector.reciprocal(prob_inv[:], prob_sum[:]))
                step(nc.vector.tensor_tensor(prob_scale[:], prob_inv[:, 1:2], neg_lam[:], ALU.mult))
                step(nc.vector.tensor_scalar(score[g % 2][:, 1, 0:n], score[g % 2][:, 1, 0:n], prob_scale[:], None, ALU.mult))
                nc.vector.scalar_tensor_tensor(out=wmix[:, 0:n], in0=score[g % 2][:, 0, 0:n], scalar=prob_inv[:, 0:1],
                                               in1=score[g % 2][:, 1, 0:n], op0=ALU.mult, op1=ALU.add).then_inc(mix_ready, 1)
                split(G_GATE + g + 1, h, 4)
                attention_output(h, g)
                if g:
                    attention_transposed(h, g)
            assert step.n - base == steps_per_head
        step.turn, step.n = 0, base + HEADS * steps_per_head

        col = gate_col
        dve.wait_ge(wif_hi_ok, 1)
        nc.vector.tensor_tensor(wif_lo[:], wif_raw[:], wif_hi[:].bitcast(F32), ALU.subtract).then_inc(wif_lo_ok, 1)

        def by_tile(c):
            return c[:].rearrange("p (t h) -> p t h", h=MH)

        def gates_a():
            dve.wait_ge(if_full, 1)
            for t in range(NT):
                ins = nc.vector.tensor_tensor(gif[:, t, :], aux[0][:, cols(t, 2 * MH)], bif[:], ALU.add)
            step(ins)
            f = gif[:, :, MH:2 * MH]
            step(nc.vector.tensor_scalar(by_tile(col["neg_f"]), f, -1.0, None, ALU.mult))
            nc.vector.tensor_tensor(by_tile(col["abs_f"]), by_tile(col["neg_f"]), f, ALU.max).then_inc(abs_ready, 1)

        def gates_b():
            dve.wait_ge(soft_ready, 1)
            nc.vector.scalar_tensor_tensor(out=by_tile(col["logf"]), in0=gif[:, :, MH:2 * MH], scalar=0.0,
                                           in1=by_tile(col["ln_f"]), op0=ALU.min, op1=ALU.subtract).then_inc(logf_ready, 1)

        def gates_c():
            dve.wait_ge(cum_full, 1)
            step(nc.vector.tensor_copy(col["b"][:], aux[1][:, 0:NG]))
            step(nc.vector.tensor_copy(col["total"][:], aux[1][:, NG:2 * NG]))
            nc.vector.tensor_tensor(by_tile(col["u"]), gif[:, :, 0:MH], by_tile(col["b"]), ALU.subtract).then_inc(u_ready, 1)

        def gates_d():
            dve.wait_ge(uT_full, 1)
            step(nc.vector.tensor_copy(uT[:], aux[2][0:NG, 0:P]))
            step(nc.vector.tensor_tensor_scan(cmT[:], uT[:], uT[:], -3.0e38, ALU.max, ALU.max))
            nc.vector.tensor_scalar(diag_cm[:], ident[0:NG, 0:NG], cmT[:, P - 1:P], None, ALU.mult).then_inc(cm_ready, 1)

        def gates_e():
            dve.wait_ge(cm_full, 1)
            step(nc.vector.tensor_copy(col["u_max"][:], aux[2][:, P:P + NG]))
            step(nc.vector.memset(col["m_prev"][:], 0.0))
            for c in range(NT):
                step(nc.vector.tensor_tensor(col["m_last"][:, cols(c, MH)], col["m_prev"][:, cols(c, MH)],
                                             col["u_max"][:, cols(c, MH)], ALU.max))
                if c + 1 < NT:
                    step(nc.vector.tensor_tensor(col["m_prev"][:, cols(c + 1, MH)], col["m_last"][:, cols(c, MH)],
                                                 col["total"][:, cols(c, MH)], ALU.add))
            step(nc.vector.tensor_tensor(col["m"][:], aux[2][:, P + NG:P + 2 * NG], col["m_prev"][:], ALU.max))
            nc.vector.tensor_scalar(col["neg_m"][:], col["m"][:], -1.0, None, ALU.mult)
            nc.vector.tensor_tensor(pack[:, 0, :], col["m_prev"][:], col["m"][:], ALU.subtract)
            step(nc.vector.tensor_tensor(pack[:, 1, :], col["b"][:], col["m"][:], ALU.add))
            nc.vector.tensor_tensor(pack[:, 2, :], col["u"][:], col["m_last"][:], ALU.subtract)
            nc.vector.tensor_tensor(pack[:, 3, :], col["m_prev"][:], col["m_last"][:], ALU.subtract)
            nc.vector.tensor_scalar(pack[:, 1, :], pack[:, 1, :], -1.0, None, ALU.mult).then_inc(pack_ready, 1)

        gates_a()
        gates_b()
        split(G_MO + 1)
        gates_c()
        split(G_MO + 2)
        gates_d()
        split(G_MO + 3)
        gates_e()
        split(G_MO + 4)
        for g in range(4):
            split(G_MO + 5 + g)
            for k in (2 * g, 2 * g + 1):
                dve.wait_ge(att_hi, k + 1)
                nc.vector.tensor_tensor(br_lo[:, k, :], aqT[:, k, :], br_hi[:, k, :].bitcast(F32), ALU.subtract).then_inc(att_lo, 1)

        def silu(k):
            e = sig_e[k % 2]
            dve.wait_ge(silu_exp, k + 1)
            step(nc.vector.tensor_scalar(e[:], e[:], 1.0, None, ALU.add))
            step(nc.vector.reciprocal(e[:], e[:]))
            nc.vector.scalar_tensor_tensor(out=mqkT[:, k, :], in0=mqkT[:, k, :], scalar=1.0 if k < MH else P ** -0.5,
                                           in1=e[:], op0=ALU.mult, op1=ALU.mult).then_inc(mqk_ready, 1)

        for j in range(2):
            for g in range(4):
                split(G_MQK + 4 * j + g + 1)
                if j == 1:
                    silu(g)
            for m in range(4):
                k = 4 * j + m
                dve.wait_ge(conv_first, k + 1)
                for s in range(1, CONV):
                    tap = V_TAP + 8 * (CONV - 1 - s) + k
                    ins = nc.vector.scalar_tensor_tensor(out=mqkT[:, k, s:SEQ], in0=acc[m][:, 0:SEQ - s],
                                                         scalar=vec[:, tap:tap + 1], in1=mqkT[:, k, s:SEQ],
                                                         op0=ALU.mult, op1=ALU.add)
                    if s < CONV - 1:
                        step(ins)
                    else:
                        ins.then_inc(bank_free[m], 1)
        dve.wait_ge(gate_stored, 10 * 16)
        nc.vector.memset(state[:], 0.0)
        nc.vector.memset(vaug[:, :, :, MV:MV + 1], 1.0).then_inc(state_zero, 1)
        for g in range(8):
            split(G_MV + g + 1)
            if g < 4:
                silu(4 + g)

        def unit_diag(u):
            nc.vector.tensor_scalar(diag[:], ident[:], col["neg_m"][:, u:u + 1], None, ALU.mult).then_inc(diag_ready, 1)

        def unit_first(u):
            dve.wait_ge(dqk_full, u + 1)
            if u + 1 < NG:
                unit_diag(u + 1)
            dve.wait_ge(e_ready, u + 1)
            nc.vector.tensor_scalar(kw[:], aux[0][:, 2 * P:3 * P], weight[:, 2, u:u + 1], None, ALU.mult)
            nc.vector.tensor_tensor(ew[:], ew[:], aux[0][:, P:2 * P], ALU.mult).then_inc(w_ready, 1)

        def unit_second(u):
            h = u % MH
            dve.wait_ge(inter_ready, u + 1)
            step(nc.vector.tensor_tensor(num[:], inter[:], aux[2][:, 0:MV + 1], ALU.add))
            step(nc.vector.scalar_tensor_tensor(out=den[:, 0:1], in0=num[:, MV:MV + 1], scalar=-1.0, in1=num[:, MV:MV + 1],
                                                op0=ALU.mult, op1=ALU.max))
            step(nc.vector.tensor_scalar(den[:, 1:2], den[:, 0:1], weight[:, 1, u:u + 1], None, ALU.max))
            nc.vector.reciprocal(den[:, 2:3], den[:, 1:2]).then_inc(den_ready, 1)
            dve.wait_ge(c_full, u + 1)
            nc.vector.scalar_tensor_tensor(out=state[:, h, :], in0=state[:, h, :], scalar=weight[:, 3, u:u + 1],
                                           in1=aux[3][:, 0:MV + 1], op0=ALU.mult, op1=ALU.add).then_inc(c_ready, 1)
            dve.wait_ge(h_rs_ok, u + 1)
            step(nc.vector.tensor_scalar(den[:, 3:4], den[:, 2:3], h_rs[:], MV ** 0.5, ALU.mult, ALU.mult))
            nc.vector.tensor_scalar(num[:, 0:MV], num[:, 0:MV], den[:, 3:4], None, ALU.mult).then_inc(h_ready, 1)

        def unit_output(u):
            c, h = divmod(u, MH)
            dve.wait_ge(hT_full, u + 1)
            for v, bank in ((0, aux[0]), (1, aux[3])):
                k = 2 * h + v
                nc.vector.scalar_tensor_tensor(out=hmT[:, k, cols(c)], in0=bank[:, 3 * P:4 * P],
                                               scalar=vec[:, V_ML + k:V_ML + k + 1], in1=moT[:, k, cols(c)],
                                               op0=ALU.mult, op1=ALU.mult).then_inc(hm_ready, 1)

        def attention_part(j, m):
            k = 4 * j + m
            dve.wait_ge(gate_loaded[k % 2], (k // 2 + 1) * 16)
            wait_bank(dve, B_ABR + j, m, G_ABR + 2 * j + 1)
            nc.vector.scalar_tensor_tensor(out=y1T[:, k, :], in0=gate_in[k % 2][:], scalar=1.0, in1=acc[m][:],
                                           op0=ALU.add, op1=ALU.mult).then_inc(bank_free[m], 1)

        dve.wait_ge(weight_ready, 1)
        unit_diag(0)
        dve.wait_ge(mo_loaded, 16)
        nc.vector.tensor_scalar(moT[:], moT[:], 0.5, 0.5, ALU.mult, ALU.add).then_inc(dve_step, 1)
        step.n += 1
        for g in range(8):
            a, b, j = 2 * g, 2 * g + 1, g // 2
            unit_first(a)
            split(G_ABR + g + 1)
            if g:
                unit_output(a - 1)
            else:
                dve.wait_ge(dve_step, step.n)
            unit_second(a)
            unit_first(b)
            if g % 2:
                attention_part(j, 0)
                attention_part(j, 1)
            unit_output(a)
            unit_second(b)
            if g % 2:
                attention_part(j, 2)
                attention_part(j, 3)
        unit_output(NG - 1)

        for k in range(KD // 2):
            dve.wait_ge(hm_hi, k + 1)
            nc.vector.tensor_tensor(br_lo[:, k, :], hmT[:, k, :], br_hi[:, k, :].bitcast(F32), ALU.subtract).then_inc(hm_lo, 1)
        for j in range(4):
            for g in range(2):
                split(G_MBR + 2 * j + g + 1)
            for m in range(4):
                k = 4 * j + m
                dve.wait_ge(gate_loaded[k % 2], ((KD + k) // 2 + 1) * 16)
                wait_bank(dve, B_MBR + j, m, G_MBR + 2 * j + 1)
                nc.vector.scalar_tensor_tensor(out=ysum[k % 2][:], in0=gate_in[k % 2][:], scalar=1.0, in1=acc[m][:],
                                               op0=ALU.add, op1=ALU.mult).then_inc(bank_free[m], 1)
                dve.wait_ge(bank_free[m], freed(B_MBR + j, m))
                nc.vector.tensor_tensor(ysum[k % 2][:], ysum[k % 2][:], y1T[:, k, :], ALU.add).then_inc(ys_ready, 1)
                dve.wait_ge(y_hi, k + 1)
                nc.vector.tensor_tensor(act_lo[:, k, :], ysum[k % 2][:], act_hi[:, k, :].bitcast(F32),
                                        ALU.subtract).then_inc(y_lo, 1)

        dve.wait_ge(x_again, 16)
        for j in range(4):
            for g in range(4):
                split(G_OUT + 4 * j + g + 1)
            for m in range(4):
                wait_bank(dve, B_OUT + j, m, G_OUT + 4 * j + 3)
                nc.vector.scalar_tensor_tensor(out=xs[:, m, cols(j, BLK)], in0=acc[m][:], scalar=0.5,
                                               in1=xs[:, m, cols(j, BLK)], op0=ALU.mult, op1=ALU.add).then_inc(bank_free[m], 1)
        for g in range(4):
            for k in range(4 * g, 4 * g + 4):
                transposed_lo(k, x1T_hi, aux[k % 4][:], act_lo[:, k, :], act_hi[:, k, :], V_CROSS, x1T_lo)
            split(G_CQ + g + 1)
            if g == 0:
                dve.wait_ge(x1_sq, 16)
                nc.vector.reduce_sum(c_sum[:], x_sums[:], AX).then_inc(c_stat, 1)
        dve.wait_ge(c_rs_ok, 1)
        step(nc.vector.tensor_scalar(c_scale[:], c_rs[:], P ** -0.5, None, ALU.mult))
        step(nc.vector.tensor_scalar(c_neg[:], c_scale[:], -1.0, None, ALU.mult))

        def cross_max(h):
            for half in range(2):
                dve.wait_ge(cs_full, 2 * h + half + 1)
                step(nc.vector.reduce_max(c_max[:, cols(half, 2)], aux[half][:].rearrange("p (t k) -> p t k", t=2), AX))
            nc.vector.tensor_tensor(c_nm[:], c_max[:], c_neg[:], ALU.mult).then_inc(cmax_ready, 1)

        cross_max(0)
        for h in range(CH):
            dve.wait_ge(cexp_ready, NT * (h + 1))
            step(nc.vector.reciprocal(c_inv[:], c_den[:]))
            for t in range(NT):
                nc.vector.tensor_scalar(cprob[h % 2][:, t, :], cprob[h % 2][:, t, :], c_inv[:, t:t + 1], None,
                                        ALU.mult).then_inc(cprob_ready, 1)
            if h + 1 < CH:
                cross_max(h + 1)
            dve.wait_ge(cT_full, 2 * h + 2)
            nc.vector.tensor_copy(probT[1][:], aux[3][:]).then_inc(cT_dve, 1)
            dve.wait_ge(co_hi, h + 1)
            nc.vector.tensor_tensor(coT_lo[:, h, :], acc[h][:], coT_hi[:, h, :].bitcast(F32), ALU.subtract).then_inc(bank_free[h], 1)

        def mlp_input_lo(j):
            for k in range(4 * j, 4 * j + 4):
                transposed_lo(k, x2T_hi, aux[k % 4][:], act_lo[:, k, :], act_hi[:, k, :], V_MLP, x2T_lo)

        for j in range(4):
            split(G_CO + j + 1)
            if j:
                mlp_input_lo(j - 1)
            for m in range(4):
                wait_bank(dve, B_CO + j, m, G_CO + j)
                nc.vector.tensor_tensor(xs[:, m, cols(j, BLK)], acc[m][:], xs[:, m, cols(j, BLK)], ALU.add).then_inc(bank_free[m], 1)
        mlp_input_lo(3)
        dve.wait_ge(x2_sq, 16)
        step(nc.vector.reduce_sum(m_sum[:], x_sums[:], AX))
        step(nc.vector.tensor_scalar(m_var[:], m_sum[:], 1.0 / D, EPS, ALU.mult, ALU.add))
        step(nc.vector.reciprocal(m_inv[:], m_var[:]))

        def hidden_lo(i, k):
            dve.wait_ge(hid_hi, i * FF_TILES + (k + 1))
            nc.vector.tensor_tensor(br_lo[:, k, :], sq_t[k % 2][:], br_hi[:, k, :].bitcast(F32), ALU.subtract).then_inc(hid_lo, 1)

        def ff_chunk(i, last=False):
            for j in range(2):
                for g in range(4):
                    split(G_FF + 4 * j + g + 1, i, FF_GR)
                for k in range(4 * j, 4 * j + 4):
                    if k >= 2:
                        dve.wait_ge(hid_lo, i * FF_TILES + (k - 1))
                    dve.wait_ge(relu_ready, i * FF_TILES + (k + 1))
                    nc.vector.tensor_tensor(sq_t[k % 2][:], relu_t[k % 2][:], acc[k % 4][:], ALU.mult).then_inc(bank_free[k % 4], 1)
                    if k % 4:
                        hidden_lo(i, k - 1)
                hidden_lo(i, 4 * j + 3)
            for j in range(4):
                for g in range(2):
                    if not (last and (j, g) == (3, 1)):
                        split(G_FF + 8 + 2 * j + g + 1, i, FF_GR)
                for m in range(4):
                    if m < 3:
                        wait_bank(dve, B_FF + 2 + j, m, 0, i * FF_BLK)
                    else:
                        dve.wait_ge(granule_used, i * FF_GR + (G_FF + 8 + 2 * j + 2))
                    nc.vector.scalar_tensor_tensor(out=xs[:, m, cols(j, BLK)], in0=acc[m][:], scalar=m_inv[:, m:m + 1],
                                                   in1=xs[:, m, cols(j, BLK)], op0=ALU.mult, op1=ALU.add).then_inc(bank_free[m], 1)

        with dve.Fori(0, N_FF - 1) as i:
            ff_chunk(i)
        ff_chunk(N_FF - 1, last=True)
        dve.wait_ge(x3_sq, N_FF * 16)
        nc.vector.reduce_sum(f_sum[:], x_sums[:], AX).then_inc(f_stat, 1)
        dve.wait_ge(fin_loaded, 16)
        dve.wait_ge(f_rs_ok, 1)
        for t in range(NT):
            nc.vector.scalar_tensor_tensor(out=xs[:, t, :], in0=xs[:, t, :], scalar=f_rs[:, t:t + 1], in1=gain_f[:],
                                           op0=ALU.mult, op1=ALU.mult).then_inc(out_ready, 1)

    @block.tensor
    def _(pe):
        def product(blk, n, granules, operands, turn=0, blk_per=1, n_per=0, banks=4, width=BLK, hooks=None, inputs=None):
            hooks = hooks or {}
            for g in range(granules):
                for piece in hooks.get((g, 0), ()):
                    piece()
                if inputs:
                    inputs(g)
                pe.wait_ge(hi_ready, turn * n_per + (n + g + 1))
                pe.wait_ge(lo_ready, turn * n_per + (n + g + 1))
                slot = (n + g) % 2
                for m in range(banks):
                    if g == 0 and blk + m > 0 and uses_before(blk, m) > 0:
                        pe.wait_ge(bank_free[m], turn * blk_per + uses_before(blk, m))
                    for k in range(GR):
                        s_hi, s_lo, v_hi, v_lo = operands(m, GR * g + k, slot, k)
                        first, last = g == 0 and k == 0, g == granules - 1 and k == GR - 1
                        dst = acc[m][:, 0:width]
                        nc.tensor.matmul(dst, s_hi, v_hi, start=first, stop=False)
                        nc.tensor.matmul(dst, s_hi, v_lo, start=False, stop=False)
                        ins = nc.tensor.matmul(dst, s_lo, v_hi, start=False, stop=last)
                    if m == banks - 1:
                        ins.then_inc(granule_used, 1)
                    elif g == granules - 1:
                        ins.then_inc(bank_full, 1)
                    for piece in hooks.get((g, m + 1), ()):
                        piece()

        def features(a_hi, a_lo):
            return lambda m, k, s, i: (whi[s][:, i, cols(m)], wlo[s][:, i, cols(m)], a_hi[:, k, :], a_lo[:, k, :])

        def tokens(a_hi, a_lo):
            return lambda m, k, s, i: (a_hi[:, k, cols(m)], a_lo[:, k, cols(m)], whi[s][:, i, :], wlo[s][:, i, :])

        def transposes(src, tiles, k, full):
            for t in range(tiles):
                ins = nc.tensor.transpose(aux[k % 4][:, cols(t)], src[:, t, cols(k)], ident[:])
            ins.then_inc(full, 1)

        pe.wait_ge(vec_loaded, 8 * 16)
        pe.wait_ge(pool_const, 1)
        nc.tensor.transpose(aux[3][:, 0:N_VEC], vec_rows[0:N_VEC, :], ident[0:N_VEC, 0:N_VEC]).then_inc(vec_full, 1)
        pe.wait_ge(mem_scaled, MT)
        pe.wait_ge(vec_ready, 1)
        for k in range(KD):
            if k >= 4:
                pe.wait_ge(memT_hi_ok, k - 3)
                pe.wait_ge(memT_lo_ok, k - 3)
            transposes(mem_sb, MT, k, memT_full)

        def memory_input(g):
            pe.wait_ge(memT_hi_ok, GR * g + GR)
            pe.wait_ge(memT_lo_ok, GR * g + GR)

        product(B_CKV, G_CKV, 4, features(memT_hi, memT_lo), width=MEM, inputs=memory_input)

        def mixer_input(k):
            def piece():
                pe.wait_ge(x_scaled, NT)
                if k >= 4:
                    pe.wait_ge(xT_hi_ok, k - 3)
                    pe.wait_ge(xT_lo_ok, k - 3)
                transposes(xs, NT, k, xT_full)
            return piece

        product(B_CKV + 1, G_CKV + 4, 4, tokens(memT_hi, memT_lo), banks=MT,
                hooks={(g, p): [mixer_input(4 * g + 2 * p), mixer_input(4 * g + 2 * p + 1)] for g in range(4) for p in range(2)})
        pe.wait_ge(xT_hi_ok, KD)
        pe.wait_ge(xT_lo_ok, KD)
        pe.wait_ge(lam_val, 1)
        pe.wait_ge(pool_const, 2)
        nc.tensor.matmul(aux[0][:, 0:1], ones[0:1, :], lam_s[0:1, 1:2], start=True, stop=True).then_inc(lam_full, 1)

        mixer = (act_hi, act_lo)
        with pe.Fori(0, 4) as i:
            product(B_QK, G_QK, 4, features(*mixer), turn=i, n_per=4)
        with pe.Fori(0, 2) as i:
            product(B_V, G_V, 4, tokens(*mixer), turn=i, n_per=4)

        def head_pieces(h):
            def scores(g):
                def piece():
                    n = (g + 1) * P
                    if g == 0:
                        pe.wait_ge(qh_ready, h + 1)
                    for mp in range(2):
                        half = slice(mp * QK, (mp + 1) * QK)
                        ins = nc.tensor.matmul(aux[mp][:, 0:n], qh[half, cols(g)], kh[half, 0:n], start=True, stop=True)
                    ins.then_inc(scores_full, 1)
                return piece

            def mix_transposes(g):
                def piece():
                    pe.wait_ge(mix_ready, h * NT + (g + 1))
                    for t in range(g + 1):
                        ins = nc.tensor.transpose(aux[2][:, cols(t)], wmix[:, cols(t)], ident[:])
                    ins.then_inc(mixT_full, 1)
                return piece

            def values(g):
                def piece():
                    pe.wait_ge(mixT_ready, h * NT + (g + 1))
                    for t in range(g + 1):
                        ins = nc.tensor.matmul(aux[3][:, 0:P], wmixT[:, cols(t)], av[:, t, ds(h * P, P)],
                                               start=t == 0, stop=t == g)
                    ins.then_inc(att_full, 1)
                return piece

            def output_transpose(g):
                def piece():
                    pe.wait_ge(att_scaled, h * NT + (g + 1))
                    nc.tensor.transpose(aux[3][:, P:2 * P], o_sb[:], ident[:]).then_inc(attT_full, 1)
                return piece

            hooks = {(0, 1): [scores(0)], (0, 3): [mix_transposes(0)], (0, 4): [values(0)], (1, 1): [output_transpose(0)]}
            for g in range(1, NT):
                hooks[g, 0] = [scores(g)]
                hooks[g, 2] = [mix_transposes(g)]
                hooks[g, 3] = [values(g)]
                hooks[g, 4] = [output_transpose(g)]
            return hooks

        with pe.Fori(0, HEADS) as h:
            product(B_GATE, G_GATE, 4, features(*mixer), turn=h, n_per=4, hooks=head_pieces(h))

        pe.wait_ge(wif_hi_ok, 1)
        pe.wait_ge(wif_lo_ok, 1)
        for t in range(NT):
            for k in range(KD):
                dst = aux[0][:, cols(t, 2 * MH)]
                nc.tensor.matmul(dst, act_hi[:, k, cols(t)], wif_hi[:, k, :], start=k == 0, stop=False)
                nc.tensor.matmul(dst, act_hi[:, k, cols(t)], wif_lo[:, k, :], start=False, stop=False)
                ins = nc.tensor.matmul(dst, act_lo[:, k, cols(t)], wif_hi[:, k, :], start=False, stop=k == KD - 1)
        ins.then_inc(if_full, 1)

        def cumulate():
            pe.wait_ge(logf_ready, 1)
            pe.wait_ge(pool_const, 5)
            nc.tensor.matmul(aux[1][:, 0:NG], tri[:], gate_col["logf"][:], start=True, stop=True)
            nc.tensor.matmul(aux[1][:, NG:2 * NG], ones[:], gate_col["logf"][:], start=True, stop=True).then_inc(cum_full, 1)

        def u_transpose():
            pe.wait_ge(u_ready, 1)
            nc.tensor.transpose(aux[2][0:NG, 0:P], gate_col["u"][:], ident[:]).then_inc(uT_full, 1)

        def maxima():
            pe.wait_ge(cm_ready, 1)
            nc.tensor.matmul(aux[2][:, P:P + NG], ones[0:NG, :], diag_cm[:], start=True, stop=True)
            nc.tensor.transpose(aux[2][:, P + NG:P + 2 * NG], cmT[:], ident[0:NG, 0:NG]).then_inc(cm_full, 1)

        product(B_MO, G_MO, 4, features(*mixer), hooks={(0, 2): [cumulate], (1, 1): [u_transpose], (2, 1): [maxima]})
        product(B_MO + 1, G_MO + 4, 4, features(*mixer))
        with pe.Fori(0, 2) as i:
            product(B_MQK, G_MQK, 4, features(*mixer), turn=i, n_per=4)
        with pe.Fori(0, 2) as i:
            product(B_MV, G_MV, 4, tokens(*mixer), turn=i, n_per=4)

        def unit_inner(u):
            c, h = divmod(u, MH)

            def piece():
                pe.wait_ge(diag_ready, u + 1)
                if u >= 2:
                    pe.wait_ge(hm_ready, 2 * (u - 1))
                q, k = mqkT[:, h, cols(c)], mqkT[:, MH + h, cols(c)]
                nc.tensor.matmul(aux[0][:, 0:P], ones[:], diag[:], start=True, stop=False)
                nc.tensor.matmul(aux[0][:, 0:P], ident[:], above[:], start=False, stop=True)
                nc.tensor.matmul(aux[0][:, P:2 * P], k, q, start=True, stop=True)
                nc.tensor.transpose(aux[0][:, 2 * P:3 * P], k, ident[:]).then_inc(dqk_full, 1)
            return piece

        def unit_outer(u):
            c, h = divmod(u, MH)

            def piece():
                if u >= MH:
                    pe.wait_ge(c_ready, u - MH + 1)
                nc.tensor.matmul(aux[1][:, 0:MV + 1], mqkT[:, h, cols(c)], state[:, h, :], start=True, stop=True)
                pe.wait_ge(w_ready, u + 1)
                nc.tensor.matmul(aux[2][:, 0:MV + 1], ew[:], vaug[:, c, h, :], start=True, stop=True).then_inc(n_full, 1)
                if u:
                    pe.wait_ge(hm_ready, 2 * u)
                nc.tensor.matmul(aux[3][:, 0:MV + 1], kw[:], vaug[:, c, h, :], start=True, stop=True).then_inc(c_full, 1)
            return piece

        def unit_transposes(u):
            def piece():
                pe.wait_ge(h_ready, u + 1)
                pe.wait_ge(w_ready, min(u + 2, NG))
                nc.tensor.transpose(aux[0][:, 3 * P:4 * P], num[:, 0:P], ident[:])
                nc.tensor.transpose(aux[3][:, 3 * P:4 * P], num[:, P:2 * P], ident[:]).then_inc(hT_full, 1)
            return piece

        pe.wait_ge(mqk_ready, 2 * MH)
        pe.wait_ge(state_zero, 1)
        pe.wait_ge(bank_free[3], freed(B_MV + 1, 3))
        pe.wait_ge(att_hi, HEADS)
        pe.wait_ge(att_lo, HEADS)
        for j in range(4):
            hooks = {}
            for g in range(2):
                a = 4 * j + 2 * g
                hooks[g, 0] = [unit_inner(a)]
                hooks[g, 1] = ([unit_transposes(a - 1)] if a else []) + [unit_outer(a)]
                hooks[g, 2] = [unit_inner(a + 1)]
                hooks[g, 3] = [unit_transposes(a), unit_outer(a + 1)]
            if j == 3:
                hooks[1, 4] = [unit_transposes(NG - 1)]
            product(B_ABR + j, G_ABR + 2 * j, 2, features(br_hi, br_lo), hooks=hooks)

        def waits(hi, lo, turn=0, per=0):
            def inputs(g):
                pe.wait_ge(hi, turn * per + GR * (g + 1))
                pe.wait_ge(lo, turn * per + GR * (g + 1))
            return inputs

        for j in range(4):
            product(B_MBR + j, G_MBR + 2 * j, 2, features(br_hi, br_lo), inputs=waits(hm_hi, hm_lo))
        with pe.Fori(0, 4) as i:
            product(B_OUT, G_OUT, 4, tokens(act_hi, act_lo), turn=i, n_per=4, inputs=waits(y_hi, y_lo))

        def residual_transposes(k, blk, full, hi, lo):
            def piece():
                for m in range(4):
                    pe.wait_ge(bank_free[m], freed(blk + k // 4, m))
                if k >= 4:
                    pe.wait_ge(hi, k - 3)
                    pe.wait_ge(lo, k - 3)
                transposes(xs, NT, k, full)
            return piece

        def x1_tile(k):
            return residual_transposes(k, B_OUT, x1T_full, x1T_hi, x1T_lo)

        hooks = {(0, 0): [x1_tile(k) for k in range(4)]}
        for g in range(3):
            for m in range(4):
                hooks[g, m + 1] = [x1_tile(4 * (g + 1) + m)]
        product(B_CQ, G_CQ, 4, features(act_hi, act_lo), inputs=waits(x1T_hi, x1T_lo), hooks=hooks)

        def cross_scores(h):
            if h == 0:
                for m in range(4):
                    pe.wait_ge(bank_free[m], freed(B_CQ, m))
                pe.wait_ge(x1T_lo, KD)
            else:
                pe.wait_ge(cexp_ready, NT * h)
            for t in range(NT):
                ins = nc.tensor.matmul(aux[t // 2][:, cols(t % 2, MEM)], cqT[:, h, cols(t)], ckT[:, h, :], start=True, stop=True)
                if t % 2:
                    ins.then_inc(cs_full, 1)

        cross_scores(0)
        for h in range(CH):
            for half in range(MT):
                pe.wait_ge(cprob_ready, NT * (h + 1))
                for t in range(NT):
                    ins = nc.tensor.transpose(aux[2 + half][:, cols(t)], cprob[h % 2][:, t, cols(half)], ident[:])
                ins.then_inc(cT_full, 1)
            if h + 1 < CH:
                cross_scores(h + 1)
            pe.wait_ge(cT_act, h + 1)
            nc.tensor.matmul(acc[h][:], cv[:, 0, cols(h)], probT[0][:], start=True, stop=False)
            pe.wait_ge(cT_dve, h + 1)
            nc.tensor.matmul(acc[h][:], cv[:, 1, cols(h)], probT[1][:], start=False, stop=True).then_inc(co_full, 1)

        def x2_tile(k):
            return residual_transposes(k, B_CO, x2T_full, x2T_hi, x2T_lo)

        for m in range(4):
            pe.wait_ge(bank_free[m], freed(B_CROSS, m))
        for j in range(4):
            hooks = {(0, m + 1): [x2_tile(4 * (j - 1) + m)] for m in range(4)} if j else {}
            product(B_CO + j, G_CO + j, 1, tokens(coT_hi, coT_lo), hooks=hooks)
        for k in range(12, 16):
            x2_tile(k)()

        with pe.Fori(0, N_FF) as i:
            for j in range(2):
                product(B_FF + j, G_FF + 4 * j, 4, features(act_hi, act_lo), turn=i, blk_per=FF_BLK, n_per=FF_GR,
                        inputs=waits(x2T_hi, x2T_lo))
            for j in range(4):
                product(B_FF + 2 + j, G_FF + 8 + 2 * j, 2, tokens(br_hi, br_lo), turn=i, blk_per=FF_BLK, n_per=FF_GR,
                        inputs=waits(hid_hi, hid_lo, i, FF_TILES))

    ctx.close()


_INS = ["x", "mem", "norm_mix", "w_in", "b_igate", "b_fgate", "conv_w", "conv_b", "lam_q1", "lam_k1", "lam_q2", "lam_k2",
        "attn_norm", "mlstm_norm", "w_attn_br", "w_mlstm_br", "w_out", "norm_cross", "norm_mem", "w_cq", "w_ckv", "w_co",
        "norm_mlp", "w_up", "w_down", "norm_final"]


def kernel(**inputs):
    import concourse.bacc as bacc
    from concourse.bass_utils import run_bass_kernel_spmd

    nc = bacc.Bacc("TRN2", target_bir_lowering=False, num_devices=1, dynamic_dma_scratch_size=1024)
    arrays, args = {}, []
    for name in _INS:
        a = np.ascontiguousarray(inputs[name])
        arrays[f"in_{name}"] = a
        args.append(nc.dram_tensor(f"in_{name}", a.shape, mybir.dt.from_np(a.dtype), kind="ExternalInput").ap())
    args.append(nc.dram_tensor("out_0", (1, SEQ, D), F32, kind="ExternalOutput").ap())
    hybrid_layer(nc, *args)
    r = run_bass_kernel_spmd(nc, [arrays], core_ids=[0])
    return r.results[0]["out_0"]
```

```python
import math
from contextlib import ExitStack

import numpy as np

import concourse.bass as bass
from concourse import mybir

F32 = mybir.dt.float32
F32R = mybir.dt.float32r
ACT = mybir.ActivationFunctionType
ALU = mybir.AluOpType
AX = mybir.AxisListType.X

P = 128
SEQ = 512
D = 2048
NT = SEQ // P
KD = D // P
MEM = 256
MT = MEM // P
HEADS = 8
QK = 64
MH = 4
MV = 256
CH = 4
CONV = 4
D_FF = 4 * D
EPS = 1e-6
LAM_INIT = 0.8 - 0.6 * math.exp(-0.3 * 0)
BLK = 512
GR = 4
FF_CHUNK = 1024
FF_TILES = FF_CHUNK // P
N_FF = D_FF // FF_CHUNK
MASKED = -1.0e30

C_Q, C_V, C_MQK, C_MV, C_MO = 0, 2048, 3072, 4096, 5120
C_IF, C_GATES = 6144, 6152

G_CKV, G_QK, G_V, G_GATE, G_MO, G_MQK, G_MV = 0, 8, 24, 32, 64, 72, 80
G_ABR, G_MBR, G_OUT, G_CQ, G_CO, G_FF = 88, 96, 104, 120, 124, 128
B_CKV, B_QK, B_V, B_GATE, B_MO, B_MQK, B_MV = 0, 2, 6, 8, 16, 18, 20
B_ABR, B_MBR, B_OUT, B_CQ, B_CO, B_FF = 22, 26, 30, 34, 35, 39
FF_GR = 2 * 4 + 4 * 2
FF_BLK = 6


def uses_before(blk, m):
    return blk - (1 if m >= 2 and blk >= 2 else 0)


def fulls_before(blk):
    return 3 * blk - (2 if blk >= 2 else 0)


class Steps:

    def __init__(self, eng, sem):
        self.eng, self.sem, self.n, self.turn = eng, sem, 0, 0

    def __call__(self, ins):
        self.n += 1
        ins.then_inc(self.sem, 1)
        self.eng.wait_ge(self.sem, self.turn + self.n)


def hybrid_layer(nc, x, mem, norm_mix, w_in, b_igate, b_fgate, conv_w, conv_b, lam_q1, lam_k1, lam_q2, lam_k2,
                 attn_norm, mlstm_norm, w_attn_br, w_mlstm_br, w_out, norm_cross, norm_mem, w_cq, w_ckv, w_co,
                 norm_mlp, w_up, w_down, norm_final, out):
    ds = bass.ds
    KB = 1024
    NG = NT * MH

    def at(name, offset, shape, dt=F32):
        return nc.alloc_sbuf_tensor_at(name, shape, dt, offset=int(offset))

    cursor = [(nc.sbuf_base + 63) // 64 * 64]

    def const(name, shape, dt=F32):
        a = at(name, cursor[0], shape, dt)
        cursor[0] += (int(np.prod(shape[1:])) * 4 + 31) // 32 * 32
        return a

    ident = const("ident", [P, P])
    tri = const("tri", [P, P])
    ones = const("ones", [P, P])
    above = const("above", [P, P])
    alibi = const("alibi", [P, SEQ])
    vec = const("vec", [P, P])
    wif_parts = const("wif_parts", [P, KD, 4 * MH], F32R)
    bif = const("bif", [P, 2 * MH])
    lam_s = const("lam_s", [1, 4])
    neg_lam = const("neg_lam", [P, 1])
    turn_mark = const("turn_mark", [P, 1])
    eps_att = const("eps_att", [P, 1])
    eps_ml = const("eps_ml", [P, 1])
    half_neg = const("half_neg", [P, 8])
    gain_att = const("gain_att", [P, 1])
    ss_mem, var_mem, rs_mem = (const(f"{n}_mem", [P, MT]) for n in ("ss", "var", "rs"))
    ss_x, var_x, rs_x = (const(f"{n}_x", [P, NT]) for n in ("ss", "var", "rs"))
    neg_max, prob_sum, prob_inv, prob_max = (const(n, [P, 2]) for n in ("neg_max", "prob_sum", "prob_inv", "prob_max"))
    prob_scale = const("prob_scale", [P, 1])
    o_ms, o_var, o_rs = (const(n, [P, 1]) for n in ("o_ms", "o_var", "o_rs"))
    gif = const("gif", [P, NT, 2 * MH])
    gate_col = {n: const(f"g_{n}", [P, NG]) for n in
                ("logf", "neg_f", "abs_f", "exp_f", "ln_f", "b", "total", "u", "m_prev", "m_last", "m", "neg_m", "u_max")}
    pack = const("pack", [P, 4, NG])
    weight = const("weight", [P, 4, NG])
    den = const("den", [P, 4])
    h_ms, h_var, h_rs = (const(n, [P, 1]) for n in ("h_ms", "h_var", "h_rs"))
    x_sums = const("x_sums", [P, NT, 4])
    c_sum, c_var, c_rs, c_scale, c_neg, m_sum, m_var, m_inv, f_sum, f_var, f_rs = (
        const(n, [P, NT]) for n in ("c_sum", "c_var", "c_rs", "c_scale", "c_neg", "m_sum", "m_var", "m_inv",
                                    "f_sum", "f_var", "f_rs"))
    c_max, c_inv = (const(n, [P, NT]) for n in ("c_max", "c_inv"))
    c_nm, c_den = (const(n, [P, 2, NT]) for n in ("c_nm", "c_den"))
    RAW = cursor[0]

    V_MIX, V_MEM, V_CROSS, V_MLP, V_TAP, V_CB, V_ATT, V_ML, N_VEC = 0, 16, 32, 48, 64, 96, 104, 105, 113

    raw = [at(f"raw{s}", RAW + s * 8 * KB, [P, GR, BLK]) for s in range(4)]
    whi = [at(f"whi{s}", RAW + (32 + 8 * s) * KB, [P, GR, BLK], F32R) for s in range(2)]
    wlo = [at(f"wlo{s}", RAW + (48 + 8 * s) * KB, [P, GR, BLK], F32R) for s in range(2)]

    A = RAW + 64 * KB
    act_hi = at("act_hi", A, [P, KD, SEQ], F32R)
    act_lo = at("act_lo", A + 32 * KB, [P, KD, SEQ], F32R)
    x_junk = [at(f"x_junk{t}", A + t * 8 * KB, [P, D]) for t in range(NT)]
    mem_junk = [at(f"mem_junk{t}", A + (32 + t * 8) * KB, [P, D]) for t in range(MT)]
    vec_rows = at("vec_rows", A + 48 * KB, [P, P])
    hmT = at("hmT", A, [P, KD // 2, SEQ])
    moT = at("moT", A + 16 * KB, [P, KD // 2, SEQ])
    y1T = at("y1T", A + 32 * KB, [P, KD, SEQ])

    R = A + 64 * KB
    memT_hi = at("memT_hi", R, [P, KD, MEM], F32R)
    memT_lo = at("memT_lo", R + 16 * KB, [P, KD, MEM], F32R)
    akT = at("akT", R, [P, HEADS, SEQ])
    av = at("av", R + 16 * KB, [P, NT, HEADS * P])
    br_hi = at("br_hi", R, [P, FF_TILES, SEQ], F32R)
    br_lo = at("br_lo", R + 16 * KB, [P, FF_TILES, SEQ], F32R)
    coT_hi = at("coT_hi", R, [P, CH, SEQ], F32R)
    coT_lo = at("coT_lo", R + 8 * KB, [P, CH, SEQ], F32R)
    cprob = [at(f"cprob{b}", R + (16 + 4 * b) * KB, [P, NT, MEM]) for b in range(2)]
    R2 = R + 32 * KB
    xs = at("xs", R2, [P, NT, D])
    aqT = at("aqT", R2, [P, HEADS, SEQ])
    vaug = at("vaug", R2, [P, NT, MH, MV + 1])
    score = [at("score0", R2 + 16 * KB, [P, 2, SEQ - P]), at("score1", R2 + 19 * KB, [P, 2, SEQ])]
    wmix = at("wmix", R2 + 23 * KB, [P, SEQ])
    wmixT = at("wmixT", R2 + 25 * KB, [P, SEQ])
    q_map = at("q_map", R2 + 27 * KB, [P, 2, SEQ], F32R)
    k_lo = at("k_lo", R2 + 31 * KB, [P, SEQ], F32R)
    o_sb = at("o_sb", R2 + 33 * KB, [P, P])
    o_junk = at("o_junk", R2 + 33 * KB + 512, [P, P])
    ifT = at("ifT", R2 + 18 * KB + 512, [4 * MH, SEQ])
    uT = at("uT", R2 + 16 * KB, [NG, P])
    cmT = at("cmT", R2 + 17 * KB, [NG, P])
    diag_cm = at("diag_cm", R2 + 18 * KB, [NG, NG])
    mqkT = at("mqkT", R2 + 16 * KB + 256, [P, 2 * MH, SEQ])
    S = R2 + 32 * KB + 256
    mem_sb = at("mem_sb", S + 4 * KB, [P, MT, D])
    junk = at("junk", S, [P, SEQ])
    rs_diag = at("rs_diag", S, [P, MT, P])
    rs_row = at("rs_row", S + 1 * KB, [P, MEM])
    lam_in = at("lam_in", S + 2 * KB, [1, 4, QK])
    lam_pr = at("lam_pr", S + 3 * KB, [1, 2, QK])
    wif_raw = at("wif_raw", S + 3 * KB + 512, [P, KD, 2 * MH])
    gate_out = at("gate_out", S + 2 * KB, [P, 4, SEQ])
    k_map = at("k_map", S + 10 * KB, [P, 2, SEQ], F32R)
    sig_e = [at(f"sig_e{b}", S + (2 + 2 * b) * KB, [P, SEQ]) for b in range(2)]
    gate_in = [at(f"gate_in{b}", S + 2 * b * KB, [P, SEQ]) for b in range(2)]
    M0 = S + 4 * KB
    ew = at("ew", M0, [P, P])
    kw = at("kw", M0 + 512, [P, P])
    diag = at("diag", M0 + 1024, [P, P])
    inter = at("inter", M0 + 1536, [P, MV + 1])
    num = at("num", M0 + 2592, [P, MV + 1])
    state = at("state", M0 + 3648, [P, MH, MV + 1])
    ysum = [at(f"ysum{b}", M0 + 2 * b * KB, [P, SEQ]) for b in range(2)]
    cqT = at("cqT", S + 2 * KB, [P, CH, SEQ])
    probT = [at("probT0", S + 10 * KB, [P, SEQ]), at("probT1", R + 24 * KB, [P, SEQ])]
    relu_t = [at(f"relu_t{b}", S + (2 + 2 * b) * KB, [P, SEQ]) for b in range(2)]
    sq_t = [at(f"sq_t{b}", S + (6 + 2 * b) * KB, [P, SEQ]) for b in range(2)]
    CK = S + 14 * KB
    ckT = at("ckT", CK, [P, CH, MEM])
    cv = at("cv", CK + 4 * KB, [P, MT, CH * P])
    gain_f = at("gain_f", S + 10 * KB, [P, D])
    assert 3648 + MH * (MV + 1) * 4 <= 9 * KB

    acc = [nc.alloc_psum_tensor(f"acc{m}", [P, BLK], F32) for m in range(4)]
    aux = [nc.alloc_psum_tensor(f"aux{m}", [P, BLK], F32) for m in range(4)]

    gates_dram = nc.dram_tensor("gates_scratch", [10, P, 4 * SEQ], F32).ap()

    sem = nc.alloc_semaphore
    vec_loaded, lam_loaded, if_loaded, fin_loaded = (
        sem(n) for n in ("vec_loaded", "lam_loaded", "if_loaded", "fin_loaded"))
    mo_loaded = [sem(f"mo_loaded{a}") for a in range(2)]
    x_again = [sem(f"x_again{j}") for j in range(4)]
    x_loaded = [sem(f"x_loaded{t}") for t in range(NT)]
    m_loaded = [sem(f"m_loaded{t}") for t in range(MT)]
    raw_loaded = [sem(f"raw_loaded{s}") for s in range(4)]
    gate_loaded = [sem(f"gate_loaded{b}") for b in range(2)]
    gate_stored, out_stored = sem("gate_stored"), sem("out_stored")
    hi_ready, lo_ready, granule_used, bank_full = (sem(n) for n in ("hi_ready", "lo_ready", "granule_used", "bank_full"))
    bank_free = [sem(f"bank_free{m}") for m in range(4)]
    dve_step, act_step, pool_step = sem("dve_step"), sem("act_step"), sem("pool_step")
    pool_const, vec_full, vec_ready, mem_ss, mem_rs, rs_diag_ok, rs_row_full, rs_row_ok, memT_full, memT_hi_ok, memT_lo_ok = (
        sem(n) for n in ("pool_const", "vec_full", "vec_ready", "mem_ss", "mem_rs", "rs_diag_ok", "rs_row_full",
                         "rs_row_ok", "memT_full", "memT_hi_ok", "memT_lo_ok"))
    x_ss, x_rs, x_scaled, xT_full, xT_hi_ok, xT_lo_ok = (
        sem(n) for n in ("x_ss", "x_rs", "x_scaled", "xT_full", "xT_hi_ok", "xT_lo_ok"))
    lam_dots, lam_exp, lam_val, lam_full, neg_lam_ok = (
        sem(n) for n in ("lam_dots", "lam_exp", "lam_val", "lam_full", "neg_lam_ok"))
    qk_hi_ok, qk_ready, scores_full, max_ready, probs_ready, mix_ready, mixT_full, mixT_ready = (
        sem(n) for n in ("qk_hi_ok", "qk_ready", "scores_full", "max_ready", "probs_ready", "mix_ready", "mixT_full", "mixT_ready"))
    att_full, att_ms, att_rs, att_scaled, attT_full, att_hi, att_lo = (
        sem(n) for n in ("att_full", "att_ms", "att_rs", "att_scaled", "attT_full", "att_hi", "att_lo"))
    wif_hi_ok, wif_lo_ok, if_full, ifT_ready, if_cols_full, abs_ready, soft_ready, logf_ready, cum_full, u_ready, uT_full, cm_ready, cm_full = (
        sem(n) for n in ("wif_hi_ok", "wif_lo_ok", "if_full", "ifT_ready", "if_cols_full", "abs_ready", "soft_ready", "logf_ready", "cum_full",
                         "u_ready", "uT_full", "cm_ready", "cm_full"))
    pack_ready, weight_ready, conv_first, silu_exp, mqk_ready, vaug_ones = (
        sem(n) for n in ("pack_ready", "weight_ready", "conv_first", "silu_exp", "mqk_ready", "vaug_ones"))
    diag_ready, dqk_full, masked_ready, e_ready, w_ready, n_full, c_full, c_ready = (
        sem(n) for n in ("diag_ready", "dqk_full", "masked_ready", "e_ready", "w_ready", "n_full", "c_full", "c_ready"))
    inter_ready, den_ready, h_sq, h_rs_ok, h_ready, hT_full, hm_ready, hm_hi, hm_lo = (
        sem(n) for n in ("inter_ready", "den_ready", "h_sq", "h_rs_ok", "h_ready", "hT_full", "hm_ready", "hm_hi", "hm_lo"))
    ys_ready, y_hi, y_lo, x1_sq, c_stat, c_rs_ok, x1T_full, x1T_hi, x1T_lo = (
        sem(n) for n in ("ys_ready", "y_hi", "y_lo", "x1_sq", "c_stat", "c_rs_ok", "x1T_full", "x1T_hi", "x1T_lo"))
    cs_full, cmax_ready, cexp_ready, cprob_ready, cT_full, cT_act, cT_dve, co_full, co_hi, co_lo = (
        sem(n) for n in ("cs_full", "cmax_ready", "cexp_ready", "cprob_ready", "cT_full", "cT_act", "cT_dve",
                         "co_full", "co_hi", "co_lo"))
    x2_sq, x2T_full, x2T_hi, x2T_lo, relu_ready, hid_hi, hid_lo, x3_sq, f_stat, f_rs_ok, out_ready = (
        sem(n) for n in ("x2_sq", "x2T_full", "x2T_hi", "x2T_lo", "relu_ready", "hid_hi", "hid_lo", "x3_sq",
                         "f_stat", "f_rs_ok", "out_ready"))

    def wait_bank(eng, blk, m, n_last, turn=0, per=4, last_bank=3):
        if m < last_bank:
            eng.wait_ge(bank_full, turn * 3 + (fulls_before(blk) + m + 1))
        else:
            eng.wait_ge(granule_used, turn * per + (n_last + 1))

    def freed(blk, m, turn=0):
        return turn + (uses_before(blk, m) + 1)

    def score_bank(h, half):
        return (acc if h % 2 else aux)[half]

    x_v = x[0].rearrange("(t p) d -> p t d", p=P)
    mem_v = mem[0].rearrange("(t p) d -> p t d", p=P)
    out_v = out[0].rearrange("(t p) d -> p t d", p=P)

    def rows(w):
        return w[0].rearrange("(k p) n -> p k n", p=P)

    w_in_v, w_abr_v, w_mbr_v, w_out_v = rows(w_in), rows(w_attn_br), rows(w_mlstm_br), rows(w_out)
    w_cq_v, w_ckv_v, w_co_v, w_up_v, w_down_v = rows(w_cq), rows(w_ckv), rows(w_co), rows(w_up), rows(w_down)

    def cols(k, n=P):
        return slice(k * n, (k + 1) * n)

    ctx = ExitStack()
    block = ctx.enter_context(nc.Block())

    @block.sync
    def _(sp):
        def load(n, slot, src, turn=0, per=0):
            if n >= 4:
                sp.wait_ge(lo_ready, turn * per + (n - 3))
            sp.dma_start(raw[slot][:], src).then_inc(raw_loaded[slot], 16)

        for t in range(MT):
            sp.dma_start(mem_sb[:, t, :], mem_v[:, t, :]).then_inc(m_loaded[t], 16)
        for first, count, src in ((V_MIX, 16, norm_mix), (V_MEM, 16, norm_mem), (V_CROSS, 16, norm_cross),
                                  (V_MLP, 16, norm_mlp), (V_CB, 8, conv_b), (V_ATT, 1, attn_norm), (V_ML, 8, mlstm_norm)):
            sp.dma_start(vec_rows[first:first + count, :], src.rearrange("a (k p) -> (a k) p", p=P)).then_inc(vec_loaded, 16)
        sp.dma_start(vec_rows[V_TAP:V_TAP + 32, :], conv_w[0].rearrange("w (k p) -> (w k) p", p=P)).then_inc(vec_loaded, 16)
        def load_x(t):
            sp.dma_start(xs[:, t, :], x_v[:, t, :]).then_inc(x_loaded[t], 16)

        for g in range(4):
            load(G_CKV + g, g, w_ckv_v[:, GR * g:GR * g + GR, 0:BLK])
            if g:
                load_x(g - 1)
        load_x(NT - 1)
        for g in range(4):
            load(G_CKV + 4 + g, g, w_ckv_v[:, GR * g:GR * g + GR, BLK:2 * BLK])
        for k, v in enumerate((lam_q1, lam_k1, lam_q2, lam_k2)):
            sp.dma_start(lam_in[0:1, k, :], v).then_inc(lam_loaded, 16)
        sp.dma_start(wif_raw[:], w_in_v[:, :, C_IF:C_IF + 2 * MH]).then_inc(if_loaded, 16)
        sp.dma_start(bif[:, 0:MH], b_igate[0].partition_broadcast(P)).then_inc(if_loaded, 16)
        sp.dma_start(bif[:, MH:2 * MH], b_fgate[0].partition_broadcast(P)).then_inc(if_loaded, 16)

        def wide_blocks(w, first_granule, first_column, first, blocks):
            with sp.Fori(first, blocks) as i:
                for g in range(4):
                    load(first_granule + g, g, w[:, GR * g:GR * g + GR, ds(i * BLK + first_column, BLK)], turn=i, per=4)

        wide_blocks(w_in_v, G_QK, C_Q, 0, 4)
        wide_blocks(w_in_v, G_V, C_V, 0, 2)
        wide_blocks(w_in_v, G_GATE, C_GATES, 0, 8)
        wide_blocks(w_in_v, G_MO, C_MO, 0, 2)
        wide_blocks(w_in_v, G_MQK, C_MQK, 0, 2)
        wide_blocks(w_in_v, G_MV, C_MV, 0, 2)

        def gate_tile(k):
            if 2 <= k < KD + 2:
                sp.wait_ge(bank_free[(k - 2) % 4], freed(B_ABR + (k - 2) // 4, (k - 2) % 4))
            elif k >= KD + 2:
                sp.wait_ge(ys_ready, k - 1 - KD)
            sp.dma_start(gate_in[k % 2][:], gates_dram[k // 4, :, cols(k % 4, SEQ)]).then_inc(gate_loaded[k % 2], 16)

        def residual(j):
            sp.dma_start(xs[:, :, cols(j, BLK)], x_v[:, :, cols(j, BLK)]).then_inc(x_again[j], 16)

        for g in range(2):
            load(G_ABR + g, g, w_abr_v[:, GR * g:GR * g + GR, 0:BLK])
        sp.wait_ge(gate_stored, 10 * 16)
        sp.wait_ge(granule_used, G_ABR)
        for a in range(2):
            sp.dma_start(moT[:, 4 * a:4 * a + 4, :].rearrange("p k t -> p (k t)"), gates_dram[8 + a]).then_inc(mo_loaded[a], 16)
        gate_tile(0)
        gate_tile(1)
        for j in range(1, 8):
            w, jj = (w_abr_v, j) if j < 4 else (w_mbr_v, j - 4)
            for g in range(2):
                load(G_ABR + 2 * j + g, (2 * j + g) % 4, w[:, GR * g:GR * g + GR, cols(jj, BLK)])
            if j == 6:
                sp.wait_ge(hm_lo, KD // 2)
            if j >= 6:
                residual(j - 6)
            for m in range(4):
                gate_tile(4 * (j - 1) + m + 2)
        for g in range(2):
            load(G_OUT + g, g, w_out_v[:, GR * g:GR * g + GR, 0:BLK])
        gate_tile(30)
        gate_tile(31)
        for g in range(2, 4):
            load(G_OUT + g, g, w_out_v[:, GR * g:GR * g + GR, 0:BLK])
            residual(g)
        wide_blocks(w_out_v, G_OUT, 0, 1, 4)
        for g in range(4):
            load(G_CQ + g, g, w_cq_v[:, GR * g:GR * g + GR, :])
        for j in range(4):
            load(G_CO + j, j, w_co_v[:, :, cols(j, BLK)])
        sp.wait_ge(co_lo, CH)
        sp.dma_start(gain_f[:], norm_final.partition_broadcast(P)).then_inc(fin_loaded, 16)
        with sp.Fori(0, N_FF) as i:
            for j in range(2):
                for g in range(4):
                    load(G_FF + 4 * j + g, g, w_up_v[:, GR * g:GR * g + GR, ds(i * FF_CHUNK + BLK * j, BLK)],
                         turn=i, per=FF_GR)
            for j in range(4):
                for g in range(2):
                    load(G_FF + 8 + 2 * j + g, (2 * j + g) % 4,
                         w_down_v[:, ds(i * FF_TILES + GR * g, GR), cols(j, BLK)], turn=i, per=FF_GR)
        for t in range(NT):
            for half in range(2):
                sp.wait_ge(out_ready, 2 * t + half + 1)
                sp.dma_start(out_v[:, t, cols(half, D // 2)], xs[:, t, cols(half, D // 2)]).then_inc(out_stored, 16)
        sp.wait_ge(out_stored, 2 * NT * 16)

    @block.gpsimd
    def _(pool):
        step = Steps(pool, pool_step)
        step(nc.gpsimd.memset(ident[:], 0.0))
        nc.gpsimd.affine_select(out=ident[:], in_=ident[:], compare_op=ALU.not_equal, fill=1.0, base=0,
                                pattern=[[-1, P]], channel_multiplier=1).then_inc(pool_const, 1)
        nc.gpsimd.memset(eps_att[:], P * EPS)
        nc.gpsimd.memset(eps_ml[:], MV * EPS)
        step(nc.gpsimd.memset(half_neg[:], -0.5))
        nc.gpsimd.memset(ones[:], 1.0).then_inc(pool_const, 1)
        step(nc.gpsimd.memset(tri[:], 1.0))
        nc.gpsimd.affine_select(out=tri[:], in_=tri[:], compare_op=ALU.is_ge, fill=0.0, base=0,
                                pattern=[[1, P]], channel_multiplier=-1).then_inc(pool_const, 1)
        step(nc.gpsimd.memset(above[:], 0.0))
        nc.gpsimd.affine_select(out=above[:], in_=above[:], compare_op=ALU.is_ge, fill=MASKED, base=0,
                                pattern=[[1, P]], channel_multiplier=-1).then_inc(pool_const, 1)
        inv = int(QK ** 0.5)
        step(nc.gpsimd.iota(alibi[:], pattern=[[inv, SEQ]], base=-inv * (SEQ - P), channel_multiplier=-inv,
                            allow_small_or_imprecise_dtypes=True))
        nc.gpsimd.affine_select(out=alibi[:], in_=alibi[:], compare_op=ALU.is_ge, fill=MASKED, base=SEQ - P,
                                pattern=[[-1, SEQ]], channel_multiplier=1).then_inc(pool_const, 1)

        def inv_rms(out_ap, var, sums, width, done):
            step(nc.gpsimd.tensor_scalar(var, sums, 1.0 / width, EPS, ALU.mult, ALU.add))
            nc.gpsimd.tensor_tensor(out_ap, var, half_neg[:, 0:var.shape[1]], ALU.pow).then_inc(done, 1)

        for t in range(MT):
            pool.wait_ge(mem_ss, t + 1)
            inv_rms(rs_mem[:, t:t + 1], var_mem[:, t:t + 1], ss_mem[:, t:t + 1], D, mem_rs)
        for t in range(NT):
            pool.wait_ge(x_ss, t + 1)
            inv_rms(rs_x[:, t:t + 1], var_x[:, t:t + 1], ss_x[:, t:t + 1], D, x_rs)

        def inv_rms_loop(turns, sums, eps, var, out_ap, ready, done):
            base = step.n
            with pool.Fori(0, turns) as i:
                step.turn = i
                pool.wait_ge(ready, i + 1)
                step(nc.gpsimd.tensor_tensor(var[:], sums[:], eps[:], ALU.add))
                nc.gpsimd.tensor_tensor(out_ap[:], var[:], half_neg[:, 0:1], ALU.pow).then_inc(done, 1)
            step.turn, step.n = 0, base + turns

        inv_rms_loop(HEADS * NT, o_ms, eps_att, o_var, o_rs, att_ms, att_rs)
        inv_rms_loop(NG, h_ms, eps_ml, h_var, h_rs, h_sq, h_rs_ok)
        pool.wait_ge(c_stat, 1)
        inv_rms(c_rs[:], c_var[:], c_sum[:], D, c_rs_ok)
        for t in range(NT):
            pool.wait_ge(f_stat, t + 1)
            inv_rms(f_rs[:, t:t + 1], f_var[:, t:t + 1], f_sum[:, t:t + 1], D, f_rs_ok)

    @block.scalar
    def _(act):
        step = Steps(act, act_step)

        def split(n, turn=0, per=0):
            act.wait_ge(raw_loaded[n % 4], turn * (per * 4) + (n // 4 + 1) * 16)
            if n >= 2:
                act.wait_ge(granule_used, turn * per + (n - 1))
            nc.scalar.activation(whi[n % 2][:], raw[n % 4][:], ACT.Copy).then_inc(hi_ready, 1)

        def evac(blk, m, n_last, dst, src, turn=0, last_bank=3):
            wait_bank(act, blk, m, n_last, turn, last_bank=last_bank)
            nc.scalar.activation(dst, src, ACT.Copy).then_inc(bank_free[m], 1)

        def transposed_hi(k, full, bank, dst, gain, done):
            act.wait_ge(full, k + 1)
            nc.scalar.activation(dst, bank, ACT.Identity, scale=vec[:, gain + k:gain + k + 1]).then_inc(done, 1)

        def memory_squares(t):
            act.wait_ge(m_loaded[t], 16)
            nc.scalar.activation(mem_junk[t][:], mem_sb[:, t, :], ACT.Square, accum_out=ss_mem[:, t:t + 1]).then_inc(mem_ss, 1)

        def memory_hi(first):
            for k in range(first, first + 4):
                transposed_hi(k, memT_full, aux[k % 4][:, 0:MEM], memT_hi[:, k, :], V_MEM, memT_hi_ok)

        def x_squares(t):
            act.wait_ge(x_loaded[t], 16)
            nc.scalar.activation(x_junk[t][:], xs[:, t, :], ACT.Square, accum_out=ss_x[:, t:t + 1]).then_inc(x_ss, 1)

        memory_squares(0)
        act.wait_ge(vec_ready, 1)
        memory_hi(0)
        split(G_CKV)
        memory_hi(4)
        memory_squares(1)
        split(G_CKV + 1)
        memory_hi(8)
        x_squares(0)
        split(G_CKV + 2)
        memory_hi(12)
        x_squares(1)
        split(G_CKV + 3)
        x_squares(2)
        x_squares(3)
        split(G_CKV + 4)
        for g in range(4):
            for k in range(4 * g, 4 * g + 4):
                transposed_hi(k, xT_full, aux[k % 4][:], act_hi[:, k, :], V_MIX, xT_hi_ok)
                if k % 4 == 1:
                    split(G_CKV + 5 + g)
        for m in range(MT):
            wait_bank(act, B_CKV + 1, m, G_CKV + 7, last_bank=1)
            nc.scalar.activation(cv[:, m, :], acc[m][:], ACT.Identity, scale=rs_mem[:, m:m + 1]).then_inc(bank_free[m], 1)
        act.wait_ge(lam_dots, 1)
        nc.scalar.activation(lam_s[0:1, 2:4], lam_s[0:1, 0:2], ACT.Exp).then_inc(lam_exp, 1)

        def score_operands_hi(h, first=False):
            if not first:
                act.wait_ge(scores_full, h * NT)
            for mp in range(2):
                half = slice(mp * QK, (mp + 1) * QK)
                nc.scalar.activation(k_map[half, mp, :], akT[half, ds(h, 1), :].rearrange("p a t -> p (a t)"), ACT.Copy)
                ins = nc.scalar.activation(q_map[half, mp, :], aqT[half, ds(h, 1), :].rearrange("p a t -> p (a t)"), ACT.Copy)
            ins.then_inc(qk_hi_ok, 1)

        def plain_blocks(blk, n, count, dst):
            with act.Fori(0, count) as i:
                for g in range(4):
                    split(n + g + 1, i, 4)
                for m in range(4):
                    evac(blk, m, n + 3, dst(i, m), acc[m][:], turn=i)

        plain_blocks(B_QK, G_QK, 2, lambda i, m: aqT[:, ds(i * 4 + m, 1), :])
        plain_blocks(B_QK + 2, G_QK + 8, 2, lambda i, m: akT[:, ds(i * 4 + m, 1), :])
        score_operands_hi(0, first=True)
        plain_blocks(B_V, G_V, 2, lambda i, m: av[:, m, ds(i * BLK, BLK)])

        act.wait_ge(if_loaded, 48)
        nc.scalar.activation(wif_parts[:, :, 0:2 * MH], wif_raw[:], ACT.Copy).then_inc(wif_hi_ok, 1)

        def gate_evac(blk, m, n_last, turn):
            wait_bank(act, blk, m, n_last, turn)
            nc.scalar.activation(gate_out[:, m, :], acc[m][:], ACT.Tanh, scale=0.5).then_inc(bank_free[m], 1)

        def gate_store(blk, turn, first):
            act.wait_ge(bank_free[3], freed(blk, 3, turn))
            act.dma_start(gates_dram[ds(turn + first, 1)].rearrange("a p n -> p (a n)"),
                          gate_out[:].rearrange("p k t -> p (k t)")).then_inc(gate_stored, 16)

        def attention_head(h, first=False, last=False):
            for g in range(NT):
                n, done = (g + 1) * P, h * NT + (g + 1)
                act.wait_ge(max_ready, done)
                for mp in range(2):
                    ins = nc.scalar.activation(score[g % 2][:, mp, 0:n], score[g % 2][:, mp, 0:n], ACT.Exp,
                                               bias=neg_max[:, mp:mp + 1], scale=QK ** -0.5,
                                               accum_out=prob_sum[:, mp:mp + 1])
                ins.then_inc(probs_ready, 1)
                split(G_GATE + g + 1, h, 4)
                if g == 3:
                    if not last:
                        score_operands_hi(h + 1)
                    if not first:
                        act.wait_ge(gate_stored, h * 16)
                    gate_evac(B_GATE, 0, G_GATE + 3, h)
                act.wait_ge(mixT_full, done)
                nc.scalar.activation(wmixT[:, 0:n], aux[2][:, 0:n], ACT.Copy).then_inc(mixT_ready, 1)
                if g == 3:
                    gate_evac(B_GATE, 1, G_GATE + 3, h)
                act.wait_ge(att_full, done)
                nc.scalar.activation(o_junk[:], aux[3][:, 0:P], ACT.Square, accum_out=o_ms[:]).then_inc(att_ms, 1)
                if g == 3:
                    gate_evac(B_GATE, 2, G_GATE + 3, h)
                    gate_evac(B_GATE, 3, G_GATE + 3, h)
                    gate_store(B_GATE, h, 0)

        attention_head(0, first=True)
        with act.Fori(1, HEADS - 1) as h:
            attention_head(h)
        attention_head(HEADS - 1, last=True)

        act.wait_ge(if_full, 1)
        nc.scalar.activation(ifT[:], aux[0][0:4 * MH, :], ACT.Copy).then_inc(ifT_ready, 1)
        for j in range(2):
            for g in range(4):
                split(G_MO + 4 * j + g + 1)
                if (j, g) == (0, 0):
                    act.wait_ge(abs_ready, 1)
                    step(nc.scalar.activation(gate_col["exp_f"][:], gate_col["abs_f"][:], ACT.Exp, scale=-1.0))
                    nc.scalar.activation(gate_col["ln_f"][:], gate_col["exp_f"][:], ACT.Ln, bias=1.0).then_inc(soft_ready, 1)
                if j == 1:
                    for k in (2 * g, 2 * g + 1):
                        nc.scalar.activation(br_hi[:, k, :], aqT[:, k, :], ACT.Copy).then_inc(att_hi, 1)
            act.wait_ge(gate_stored, (8 + j) * 16)
            for m in range(4):
                gate_evac(B_MO + j, m, G_MO + 4 * j + 3, 0)
            gate_store(B_MO + j, 0, 8 + j)
            if j == 0:
                act.wait_ge(pack_ready, 1)
                nc.scalar.activation(weight[:], pack[:], ACT.Exp).then_inc(weight_ready, 1)

        def silu_exponential(k):
            act.wait_ge(bank_free[k % 4], freed(B_MQK + k // 4, k % 4))
            if k >= 2:
                act.wait_ge(mqk_ready, k - 1)
            nc.scalar.activation(sig_e[k % 2][:], mqkT[:, k, :], ACT.Exp, scale=-1.0).then_inc(silu_exp, 1)

        act.wait_ge(gate_stored, 10 * 16)
        for j in range(2):
            for g in range(4):
                split(G_MQK + 4 * j + g + 1)
                if j == 1:
                    silu_exponential(g)
            for m in range(4):
                k = 4 * j + m
                wait_bank(act, B_MQK + j, m, G_MQK + 4 * j + 3)
                nc.scalar.activation(mqkT[:, k, :], acc[m][:], ACT.Identity, scale=vec[:, V_TAP + 24 + k:V_TAP + 25 + k],
                                     bias=vec[:, V_CB + k:V_CB + k + 1]).then_inc(conv_first, 1)
        act.wait_ge(att_lo, HEADS)
        for j in range(2):
            for g in range(4):
                split(G_MV + 4 * j + g + 1)
                if j == 0:
                    silu_exponential(4 + g)
            for m in range(4):
                evac(B_MV + j, m, G_MV + 4 * j + 3, vaug[:, m, 2 * j:2 * j + 2, 0:MV],
                     acc[m][:].rearrange("p (h v) -> p h v", h=2))

        def unit_first(u):
            act.wait_ge(masked_ready, u + 1)
            nc.scalar.activation(ew[:], ew[:], ACT.Exp, bias=gate_col["u"][:, u:u + 1]).then_inc(e_ready, 1)

        def unit_second(u):
            if u >= MH:
                act.wait_ge(n_full, u + 1)
                nc.scalar.activation(inter[:], aux[1][:, 0:MV + 1], ACT.Identity,
                                     scale=weight[:, 0, u:u + 1]).then_inc(inter_ready, 1)
            act.wait_ge(den_ready, u + 1)
            nc.scalar.activation(inter[:, 0:MV], num[:, 0:MV], ACT.Square, scale=den[:, 2:3],
                                 accum_out=h_ms[:]).then_inc(h_sq, 1)

        def output_hi(k):
            act.wait_ge(hm_ready, 2 * (NG - MH + k // 2 + 1))
            nc.scalar.activation(br_hi[:, k, :], hmT[:, k, :], ACT.Copy).then_inc(hm_hi, 1)

        unit_first(0)
        for g in range(8):
            split(G_ABR + g + 1)
            unit_second(2 * g)
            unit_first(2 * g + 1)
            if g == 7:
                act.wait_ge(granule_used, G_ABR + 7)
                for k in range(GR):
                    output_hi(k)
            unit_second(2 * g + 1)
            if 2 * g + 2 < NG:
                unit_first(2 * g + 2)

        act.wait_ge(granule_used, G_ABR + 8)
        for k in range(GR, KD // 2):
            output_hi(k)
        for j in range(4):
            for g in range(2):
                split(G_MBR + 2 * j + g + 1)
            for k in range(4 * j, 4 * j + 4):
                act.wait_ge(ys_ready, k + 1)
                nc.scalar.activation(act_hi[:, k, :], ysum[k % 2][:], ACT.Copy).then_inc(y_hi, 1)

        def squares(blk, m, j, done, before, turn=0):
            act.wait_ge(bank_free[m], freed(blk, m, turn))
            if before is not None:
                act.wait_ge(done, before)
            nc.scalar.activation(junk[:], xs[:, m, cols(j, BLK)], ACT.Square, accum_out=x_sums[:, m, j:j + 1]).then_inc(done, 1)

        def query_input_hi(k):
            transposed_hi(k, x1T_full, aux[k % 4][:], act_hi[:, k, :], V_CROSS, x1T_hi)

        for j in range(4):
            for g in range(4):
                split(G_OUT + 4 * j + g + 1)
                if (j, g) == (3, 2):
                    for k in range(4):
                        query_input_hi(k)
            for m in range(4):
                if j == 3:
                    query_input_hi(4 + m)
                squares(B_OUT + j, m, j, x1_sq, 4 * j + m or None)
        for g in range(4):
            split(G_CQ + g + 1)
            if g < 2:
                for k in range(8 + 4 * g, 12 + 4 * g):
                    query_input_hi(k)
        for m in range(3):
            evac(B_CQ, m, G_CQ + 3, cqT[:, m, :], acc[m][:])

        def cross_exponentials(h):
            act.wait_ge(cmax_ready, h + 1)
            if h >= 2:
                act.wait_ge(cT_full, 2 * (h - 1))
            for t in range(NT):
                nc.scalar.activation(cprob[h % 2][:, t, :], score_bank(h, t // 2)[:, cols(t % 2, MEM)], ACT.Exp,
                                     bias=c_nm[:, h % 2, t:t + 1], scale=c_scale[:, t:t + 1],
                                     accum_out=c_den[:, h % 2, t:t + 1]).then_inc(cexp_ready, 1)

        cross_exponentials(0)
        evac(B_CQ, 3, G_CQ + 3, cqT[:, 3, :], acc[3][:])
        for h in range(CH):
            act.wait_ge(cT_full, 2 * h + 1)
            nc.scalar.activation(probT[0][:], aux[2][:], ACT.Copy).then_inc(cT_act, 1)
            if h == 0:
                cross_exponentials(1)
            if h + 2 < CH:
                cross_exponentials(h + 2)
            act.wait_ge(co_full, h + 1)
            nc.scalar.activation(coT_hi[:, h, :], acc[2 + h % 2][:], ACT.Copy).then_inc(co_hi, 1)

        def mlp_input_hi(k):
            transposed_hi(k, x2T_full, aux[k % 4][:], act_hi[:, k, :], V_MLP, x2T_hi)

        for j in range(4):
            split(G_CO + j + 1)
            for m in range(4):
                if j:
                    mlp_input_hi(4 * (j - 1) + m)
                if m:
                    squares(B_CO + j, m - 1, j, x2_sq, 4 * j + m - 1 or None)
            squares(B_CO + j, 3, j, x2_sq, 4 * j + 3)

        def hidden_hi(i, k):
            act.wait_ge(bank_free[k % 4], freed(B_FF + k // 4, k % 4, i * FF_BLK))
            nc.scalar.activation(br_hi[:, k, :], sq_t[k % 2][:], ACT.Copy).then_inc(hid_hi, 1)

        def ff_chunk(i, first=False, last=False):
            for j in range(2):
                for g in range(4):
                    split(G_FF + 4 * j + g + 1, i, FF_GR)
                    if first and (j, g) == (0, 0):
                        for k in range(12, KD):
                            mlp_input_hi(k)
                for k in range(4 * j, 4 * j + 4):
                    wait_bank(act, B_FF + j, k % 4, G_FF + 4 * j + 3, i * FF_BLK) if k % 4 < 3 else \
                        act.wait_ge(granule_used, i * FF_GR + (G_FF + 4 * j + 4))
                    nc.scalar.activation(relu_t[k % 2][:], acc[k % 4][:], ACT.Relu).then_inc(relu_ready, 1)
                    if k % 4:
                        hidden_hi(i, k - 1)
                hidden_hi(i, 4 * j + 3)
            for j in range(4):
                for g in range(2):
                    if not (last and (j, g) == (3, 1)):
                        split(G_FF + 8 + 2 * j + g + 1, i, FF_GR)
                for m in range(4):
                    k = 4 * j + m
                    squares(B_FF + 2 + j, m, j, x3_sq, None if first and k == 0 else i * 16 + k, i * FF_BLK)

        ff_chunk(0, first=True)
        with act.Fori(1, N_FF - 1) as i:
            ff_chunk(i)
        ff_chunk(N_FF - 1, last=True)

    @block.vector
    def _(dve):
        step = Steps(dve, dve_step)

        def split(n, turn=0, per=0):
            dve.wait_ge(hi_ready, turn * per + (n + 1))
            nc.vector.tensor_tensor(wlo[n % 2][:], raw[n % 4][:], whi[n % 2][:].bitcast(F32), ALU.subtract).then_inc(lo_ready, 1)

        def transposed_lo(k, hi_ok, bank, dst, hi, gain, done):
            dve.wait_ge(hi_ok, k + 1)
            nc.vector.scalar_tensor_tensor(out=dst, in0=bank, scalar=vec[:, gain + k:gain + k + 1], in1=hi.bitcast(F32),
                                           op0=ALU.mult, op1=ALU.subtract).then_inc(done, 1)

        dve.wait_ge(vec_full, 1)
        nc.vector.tensor_copy(vec[:, 0:N_VEC], aux[3][:, 0:N_VEC]).then_inc(vec_ready, 1)
        dve.wait_ge(vec_ready, 1)
        nc.vector.tensor_scalar(gain_att[:], vec[:, V_ATT:V_ATT + 1], 1.0 - LAM_INIT, None, ALU.mult)
        def memory_lo(first):
            for k in range(first, first + 4):
                transposed_lo(k, memT_hi_ok, aux[k % 4][:, 0:MEM], memT_lo[:, k, :], memT_hi[:, k, :], V_MEM, memT_lo_ok)

        def scale_x(t):
            dve.wait_ge(x_rs, t + 1)
            nc.vector.tensor_scalar(xs[:, t, :], xs[:, t, :], rs_x[:, t:t + 1], None, ALU.mult).then_inc(x_scaled, 1)

        memory_lo(0)
        split(G_CKV)
        memory_lo(4)
        split(G_CKV + 1)
        memory_lo(8)
        for t in range(MT):
            dve.wait_ge(mem_rs, t + 1)
            nc.vector.tensor_scalar(rs_diag[:, t, :], ident[:], rs_mem[:, t:t + 1], None, ALU.mult).then_inc(rs_diag_ok, 1)
        scale_x(0)
        split(G_CKV + 2)
        memory_lo(12)
        dve.wait_ge(rs_row_full, 1)
        nc.vector.tensor_copy(rs_row[:], aux[0][:, 0:MEM]).then_inc(rs_row_ok, 1)
        scale_x(1)
        split(G_CKV + 3)
        scale_x(2)
        scale_x(3)
        split(G_CKV + 4)
        dve.wait_ge(rs_row_ok, 1)
        for m in range(4):
            wait_bank(dve, B_CKV, m, G_CKV + 3)
            nc.vector.tensor_tensor(ckT[:, m, :], acc[m][:, 0:MEM], rs_row[:], ALU.mult).then_inc(bank_free[m], 1)
        for g in range(4):
            for k in range(4 * g, 4 * g + 4):
                transposed_lo(k, xT_hi_ok, aux[k % 4][:], act_lo[:, k, :], act_hi[:, k, :], V_MIX, xT_lo_ok)
                if k % 4 == 1:
                    split(G_CKV + 5 + g)
        dve.wait_ge(lam_loaded, 64)
        step(nc.vector.tensor_tensor(lam_pr[:], lam_in[0:1, 0:4:2, :], lam_in[0:1, 1:4:2, :], ALU.mult))
        nc.vector.reduce_sum(lam_s[0:1, 0:2], lam_pr[:], AX).then_inc(lam_dots, 1)
        dve.wait_ge(lam_exp, 1)
        step(nc.vector.tensor_tensor(lam_s[0:1, 0:1], lam_s[0:1, 3:4], lam_s[0:1, 2:3], ALU.subtract))
        nc.vector.tensor_scalar(lam_s[0:1, 1:2], lam_s[0:1, 0:1], -LAM_INIT, None, ALU.add).then_inc(lam_val, 1)

        def score_operands_lo(h):
            dve.wait_ge(qk_hi_ok, h + 1)
            for mp in range(2):
                half, other = slice(mp * QK, (mp + 1) * QK), slice((1 - mp) * QK, (2 - mp) * QK)
                nc.vector.tensor_tensor(k_lo[half, :], akT[half, ds(h, 1), :].rearrange("p a t -> p (a t)"),
                                        k_map[half, mp, :].bitcast(F32), ALU.subtract)
                nc.vector.tensor_tensor(q_map[other, mp, :], aqT[half, ds(h, 1), :].rearrange("p a t -> p (a t)"),
                                        q_map[half, mp, :].bitcast(F32), ALU.subtract)
                ins = nc.vector.tensor_copy(k_map[other, mp, :], k_map[half, mp, :].bitcast(F32))
            ins.then_inc(qk_ready, 1)

        with dve.Fori(0, 4) as i:
            for g in range(4):
                split(G_QK + g + 1, i, 4)
        dve.wait_ge(lam_full, 1)
        nc.vector.tensor_copy(neg_lam[:], aux[0][:, 0:1]).then_inc(neg_lam_ok, 1)
        score_operands_lo(0)
        with dve.Fori(0, 2) as i:
            for g in range(4):
                split(G_V + g + 1, i, 4)

        dve.wait_ge(wif_hi_ok, 1)
        nc.vector.tensor_tensor(wif_parts[:, :, 2 * MH:4 * MH], wif_raw[:], wif_parts[:, :, 0:2 * MH].bitcast(F32),
                                ALU.subtract).then_inc(wif_lo_ok, 1)

        dve.wait_ge(pool_const, 5)
        base = step.n

        def attention_output(h, g):
            dve.wait_ge(att_rs, h * NT + (g + 1))
            nc.vector.tensor_scalar(o_sb[:], aux[3][:, 0:P], o_rs[:], P ** 0.5, ALU.mult, ALU.mult).then_inc(att_scaled, 1)

        def attention_transposed(h, g):
            dve.wait_ge(attT_full, h * NT + (g + 1))
            nc.vector.tensor_scalar(aqT[:, ds(h, 1), cols(g)].rearrange("p a t -> p (a t)"), aux[3][:, P:2 * P], gain_att[:],
                                    None, ALU.mult)

        steps_per_head = 1 + NT * 4

        def attention_head(h, last=False):
            step.turn = h * steps_per_head
            step(nc.vector.tensor_scalar(alibi[:], alibi[:], 0.5, None, ALU.mult))
            for g in range(NT):
                n, done = (g + 1) * P, h * NT + (g + 1)
                dve.wait_ge(scores_full, done)
                nc.vector.memset(turn_mark[:], 0.0)
                nc.vector.tensor_tensor_reduce(out=score[g % 2][:, 0, 0:n], in0=aux[0][:, 0:n],
                                                in1=alibi[:, SEQ - n:SEQ], scale=1.0, scalar=-3.0e38, op0=ALU.add,
                                                op1=ALU.max, accum_out=prob_max[:, 0:1])
                step(nc.vector.tensor_tensor_reduce(out=score[g % 2][:, 1, 0:n], in0=aux[1][:, 0:n],
                                                    in1=alibi[:, SEQ - n:SEQ], scale=1.0, scalar=-3.0e38, op0=ALU.add,
                                                    op1=ALU.max, accum_out=prob_max[:, 1:2]))
                nc.vector.tensor_scalar(neg_max[:], prob_max[:], -(QK ** -0.5), None, ALU.mult).then_inc(max_ready, 1)
                if g == 1:
                    attention_transposed(h, 0)
                dve.wait_ge(probs_ready, done)
                step(nc.vector.reciprocal(prob_inv[:], prob_sum[:]))
                step(nc.vector.tensor_tensor(prob_scale[:], prob_inv[:, 1:2], neg_lam[:], ALU.mult))
                step(nc.vector.tensor_scalar(score[g % 2][:, 1, 0:n], score[g % 2][:, 1, 0:n], prob_scale[:], None, ALU.mult))
                nc.vector.scalar_tensor_tensor(out=wmix[:, 0:n], in0=score[g % 2][:, 0, 0:n], scalar=prob_inv[:, 0:1],
                                               in1=score[g % 2][:, 1, 0:n], op0=ALU.mult, op1=ALU.add).then_inc(mix_ready, 1)
                split(G_GATE + g + 1, h, 4)
                if g == 3 and not last:
                    score_operands_lo(h + 1)
                attention_output(h, g)
                if g:
                    attention_transposed(h, g)
            assert step.n - base == steps_per_head
            step.turn, step.n = 0, base

        with dve.Fori(0, HEADS - 1) as h:
            attention_head(h)
        attention_head(HEADS - 1, last=True)
        step.n = base + HEADS * steps_per_head

        col = gate_col
        def by_tile(c):
            return c[:].rearrange("p (t h) -> p t h", h=MH)

        def gates_a():
            dve.wait_ge(if_cols_full, 1)
            parts = aux[1][:, 0:NT * 4 * MH].rearrange("p (t n) -> p t n", t=NT)
            step(nc.vector.tensor_copy(gif[:], parts[:, :, 2 * MH:4 * MH]))
            step(nc.vector.tensor_tensor(gif[:], gif[:], parts[:, :, 0:2 * MH], ALU.add))
            for t in range(NT):
                ins = nc.vector.tensor_tensor(gif[:, t, :], gif[:, t, :], bif[:], ALU.add)
            step(ins)
            f = gif[:, :, MH:2 * MH]
            step(nc.vector.tensor_scalar(by_tile(col["neg_f"]), f, -1.0, None, ALU.mult))
            nc.vector.tensor_tensor(by_tile(col["abs_f"]), by_tile(col["neg_f"]), f, ALU.max).then_inc(abs_ready, 1)

        def gates_b():
            dve.wait_ge(soft_ready, 1)
            nc.vector.scalar_tensor_tensor(out=by_tile(col["logf"]), in0=gif[:, :, MH:2 * MH], scalar=0.0,
                                           in1=by_tile(col["ln_f"]), op0=ALU.min, op1=ALU.subtract).then_inc(logf_ready, 1)

        def gates_c():
            dve.wait_ge(cum_full, 1)
            step(nc.vector.tensor_copy(col["b"][:], aux[1][:, 0:NG]))
            step(nc.vector.tensor_copy(col["total"][:], aux[1][:, NG:2 * NG]))
            nc.vector.tensor_tensor(by_tile(col["u"]), gif[:, :, 0:MH], by_tile(col["b"]), ALU.subtract).then_inc(u_ready, 1)

        def gates_d():
            dve.wait_ge(uT_full, 1)
            step(nc.vector.tensor_copy(uT[:], aux[2][0:NG, 0:P]))
            step(nc.vector.tensor_tensor_scan(cmT[:], uT[:], uT[:], -3.0e38, ALU.max, ALU.max))
            nc.vector.tensor_scalar(diag_cm[:], ident[0:NG, 0:NG], cmT[:, P - 1:P], None, ALU.mult).then_inc(cm_ready, 1)

        def gates_e():
            dve.wait_ge(cm_full, 1)
            step(nc.vector.tensor_copy(col["u_max"][:], aux[2][:, P:P + NG]))
            step(nc.vector.memset(col["m_prev"][:], 0.0))
            for c in range(NT):
                step(nc.vector.tensor_tensor(col["m_last"][:, cols(c, MH)], col["m_prev"][:, cols(c, MH)],
                                             col["u_max"][:, cols(c, MH)], ALU.max))
                if c + 1 < NT:
                    step(nc.vector.tensor_tensor(col["m_prev"][:, cols(c + 1, MH)], col["m_last"][:, cols(c, MH)],
                                                 col["total"][:, cols(c, MH)], ALU.add))
            step(nc.vector.tensor_tensor(col["m"][:], aux[2][:, P + NG:P + 2 * NG], col["m_prev"][:], ALU.max))
            nc.vector.tensor_scalar(col["neg_m"][:], col["m"][:], -1.0, None, ALU.mult)
            nc.vector.tensor_tensor(pack[:, 0, :], col["m_prev"][:], col["m"][:], ALU.subtract)
            step(nc.vector.tensor_tensor(pack[:, 1, :], col["b"][:], col["m"][:], ALU.add))
            nc.vector.tensor_tensor(pack[:, 2, :], col["u"][:], col["m_last"][:], ALU.subtract)
            nc.vector.tensor_tensor(pack[:, 3, :], col["m_prev"][:], col["m_last"][:], ALU.subtract)
            nc.vector.tensor_scalar(pack[:, 1, :], pack[:, 1, :], -1.0, None, ALU.mult).then_inc(pack_ready, 1)

        split(G_MO + 1)
        gates_a()
        gates_b()
        split(G_MO + 2)
        gates_c()
        split(G_MO + 3)
        gates_d()
        split(G_MO + 4)
        gates_e()
        for g in range(4):
            split(G_MO + 5 + g)
            for k in (2 * g, 2 * g + 1):
                dve.wait_ge(att_hi, k + 1)
                nc.vector.tensor_tensor(br_lo[:, k, :], aqT[:, k, :], br_hi[:, k, :].bitcast(F32), ALU.subtract).then_inc(att_lo, 1)

        def silu(k):
            e = sig_e[k % 2]
            dve.wait_ge(silu_exp, k + 1)
            step(nc.vector.tensor_scalar(e[:], e[:], 1.0, None, ALU.add))
            step(nc.vector.reciprocal(e[:], e[:]))
            nc.vector.scalar_tensor_tensor(out=mqkT[:, k, :], in0=mqkT[:, k, :], scalar=1.0 if k < MH else P ** -0.5,
                                           in1=e[:], op0=ALU.mult, op1=ALU.mult).then_inc(mqk_ready, 1)

        for j in range(2):
            for g in range(4):
                split(G_MQK + 4 * j + g + 1)
                if j == 1:
                    silu(g)
            for m in range(4):
                k = 4 * j + m
                dve.wait_ge(conv_first, k + 1)
                for s in range(1, CONV):
                    tap = V_TAP + 8 * (CONV - 1 - s) + k
                    ins = nc.vector.scalar_tensor_tensor(out=mqkT[:, k, s:SEQ], in0=acc[m][:, 0:SEQ - s],
                                                         scalar=vec[:, tap:tap + 1], in1=mqkT[:, k, s:SEQ],
                                                         op0=ALU.mult, op1=ALU.add)
                    if s < CONV - 1:
                        step(ins)
                    else:
                        ins.then_inc(bank_free[m], 1)
        nc.vector.memset(vaug[:, :, :, MV:MV + 1], 1.0).then_inc(vaug_ones, 1)
        for g in range(8):
            split(G_MV + g + 1)
            if g < 4:
                silu(4 + g)

        def unit_diag(u):
            nc.vector.tensor_scalar(diag[:], ident[:], col["neg_m"][:, u:u + 1], None, ALU.mult).then_inc(diag_ready, 1)

        def unit_first(u):
            dve.wait_ge(dqk_full, u + 1)
            if u:
                dve.wait_ge(n_full, u)
            nc.vector.tensor_tensor(ew[:], aux[0][:, 0:P], above[:], ALU.add).then_inc(masked_ready, 1)
            if u + 1 < NG:
                unit_diag(u + 1)
            if u < NG - MH:
                nc.vector.tensor_scalar(kw[:], aux[0][:, 2 * P:3 * P], weight[:, 2, u:u + 1], None, ALU.mult)
            dve.wait_ge(e_ready, u + 1)
            nc.vector.tensor_tensor(ew[:], ew[:], aux[0][:, P:2 * P], ALU.mult).then_inc(w_ready, 1)

        def unit_second(u):
            h = u % MH
            if u < MH:
                dve.wait_ge(n_full, u + 1)
                step(nc.vector.tensor_copy(num[:], aux[2][:, 0:MV + 1]))
            else:
                dve.wait_ge(inter_ready, u - MH + 1)
                step(nc.vector.tensor_tensor(num[:], inter[:], aux[2][:, 0:MV + 1], ALU.add))
            step(nc.vector.scalar_tensor_tensor(out=den[:, 0:1], in0=num[:, MV:MV + 1], scalar=-1.0, in1=num[:, MV:MV + 1],
                                                op0=ALU.mult, op1=ALU.max))
            step(nc.vector.tensor_scalar(den[:, 1:2], den[:, 0:1], weight[:, 1, u:u + 1], None, ALU.max))
            nc.vector.reciprocal(den[:, 2:3], den[:, 1:2]).then_inc(den_ready, 1)
            if u < NG - MH:
                dve.wait_ge(c_full, u + 1)
            if u < MH:
                nc.vector.tensor_copy(state[:, h, :], aux[3][:, 0:MV + 1]).then_inc(c_ready, 1)
            elif u < NG - MH:
                nc.vector.scalar_tensor_tensor(out=state[:, h, :], in0=state[:, h, :], scalar=weight[:, 3, u:u + 1],
                                               in1=aux[3][:, 0:MV + 1], op0=ALU.mult, op1=ALU.add).then_inc(c_ready, 1)

        def unit_scale(u):
            dve.wait_ge(h_rs_ok, u + 1)
            step(nc.vector.tensor_scalar(den[:, 3:4], den[:, 2:3], h_rs[:], MV ** 0.5, ALU.mult, ALU.mult))
            nc.vector.tensor_scalar(num[:, 0:MV], num[:, 0:MV], den[:, 3:4], None, ALU.mult).then_inc(h_ready, 1)

        def unit_output(u):
            c, h = divmod(u, MH)
            dve.wait_ge(hT_full, u + 1)
            for v, bank in ((0, aux[0]), (1, aux[3])):
                k = 2 * h + v
                nc.vector.scalar_tensor_tensor(out=hmT[:, k, cols(c)], in0=bank[:, 3 * P:4 * P],
                                               scalar=vec[:, V_ML + k:V_ML + k + 1], in1=moT[:, k, cols(c)],
                                               op0=ALU.mult, op1=ALU.mult).then_inc(hm_ready, 1)

        def attention_part(j, m):
            k = 4 * j + m
            dve.wait_ge(gate_loaded[k % 2], (k // 2 + 1) * 16)
            wait_bank(dve, B_ABR + j, m, G_ABR + 2 * j + 1)
            nc.vector.scalar_tensor_tensor(out=y1T[:, k, :], in0=gate_in[k % 2][:], scalar=1.0, in1=acc[m][:],
                                           op0=ALU.add, op1=ALU.mult).then_inc(bank_free[m], 1)

        def output_lo(k):
            dve.wait_ge(hm_hi, k + 1)
            nc.vector.tensor_tensor(br_lo[:, k, :], hmT[:, k, :], br_hi[:, k, :].bitcast(F32), ALU.subtract).then_inc(hm_lo, 1)

        def output_gate(half):
            part = moT[:, 4 * half:4 * half + 4, :]
            dve.wait_ge(mo_loaded[half], 16)
            step(nc.vector.tensor_scalar(part, part, 0.5, 0.5, ALU.mult, ALU.add))

        dve.wait_ge(weight_ready, 1)
        unit_diag(0)
        unit_first(0)
        for g in range(8):
            a, b, j = 2 * g, 2 * g + 1, g // 2
            if g:
                unit_output(a - 1)
            split(G_ABR + g + 1)
            unit_second(a)
            unit_first(b)
            unit_scale(a)
            if g % 2:
                attention_part(j, 0)
                attention_part(j, 1)
            if g == 0:
                output_gate(0)
            unit_output(a)
            if g == 7:
                for k in range(GR):
                    output_lo(k)
            unit_second(b)
            if b + 1 < NG:
                unit_first(b + 1)
            unit_scale(b)
            if g == 0:
                output_gate(1)
            if g % 2:
                attention_part(j, 2)
                attention_part(j, 3)
        unit_output(NG - 1)
        for k in range(GR, KD // 2):
            output_lo(k)
        for j in range(4):
            for g in range(2):
                split(G_MBR + 2 * j + g + 1)
            for m in range(4):
                k = 4 * j + m
                dve.wait_ge(gate_loaded[k % 2], ((KD + k) // 2 + 1) * 16)
                wait_bank(dve, B_MBR + j, m, G_MBR + 2 * j + 1)
                nc.vector.scalar_tensor_tensor(out=ysum[k % 2][:], in0=gate_in[k % 2][:], scalar=1.0, in1=acc[m][:],
                                               op0=ALU.add, op1=ALU.mult).then_inc(bank_free[m], 1)
                dve.wait_ge(bank_free[m], freed(B_MBR + j, m))
                nc.vector.tensor_tensor(ysum[k % 2][:], ysum[k % 2][:], y1T[:, k, :], ALU.add).then_inc(ys_ready, 1)
                dve.wait_ge(y_hi, k + 1)
                nc.vector.tensor_tensor(act_lo[:, k, :], ysum[k % 2][:], act_hi[:, k, :].bitcast(F32),
                                        ALU.subtract).then_inc(y_lo, 1)

        def query_input_lo(k):
            transposed_lo(k, x1T_hi, aux[k % 4][:], act_lo[:, k, :], act_hi[:, k, :], V_CROSS, x1T_lo)

        for j in range(4):
            for g in range(4):
                split(G_OUT + 4 * j + g + 1)
                if (j, g) == (3, 2):
                    for k in range(4):
                        query_input_lo(k)
            for m in range(4):
                if j == 3:
                    query_input_lo(4 + m)
                if m == 0:
                    dve.wait_ge(x_again[j], 16)
                wait_bank(dve, B_OUT + j, m, G_OUT + 4 * j + 3)
                nc.vector.scalar_tensor_tensor(out=xs[:, m, cols(j, BLK)], in0=acc[m][:], scalar=0.5,
                                               in1=xs[:, m, cols(j, BLK)], op0=ALU.mult, op1=ALU.add).then_inc(bank_free[m], 1)
        for g in range(4):
            split(G_CQ + g + 1)
            if g < 2:
                for k in range(8 + 4 * g, 12 + 4 * g):
                    query_input_lo(k)
            if g == 1:
                dve.wait_ge(x1_sq, 16)
                nc.vector.reduce_sum(c_sum[:], x_sums[:], AX).then_inc(c_stat, 1)
        dve.wait_ge(c_rs_ok, 1)
        step(nc.vector.tensor_scalar(c_scale[:], c_rs[:], P ** -0.5, None, ALU.mult))
        step(nc.vector.tensor_scalar(c_neg[:], c_scale[:], -1.0, None, ALU.mult))

        def cross_max(h):
            if h:
                dve.wait_ge(cmax_ready, h)
            for half in range(2):
                dve.wait_ge(cs_full, 2 * h + half + 1)
                step(nc.vector.reduce_max(c_max[:, cols(half, 2)],
                                          score_bank(h, half)[:].rearrange("p (t k) -> p t k", t=2), AX))
            nc.vector.tensor_tensor(c_nm[:, h % 2, :], c_max[:], c_neg[:], ALU.mult).then_inc(cmax_ready, 1)

        def cross_normalize(h):
            dve.wait_ge(cexp_ready, NT * (h + 1))
            if h:
                dve.wait_ge(cprob_ready, NT * h)
            step(nc.vector.reciprocal(c_inv[:], c_den[:, h % 2, :]))
            for t in range(NT):
                nc.vector.tensor_scalar(cprob[h % 2][:, t, :], cprob[h % 2][:, t, :], c_inv[:, t:t + 1], None,
                                        ALU.mult).then_inc(cprob_ready, 1)

        def cross_output_lo(h):
            dve.wait_ge(co_hi, h + 1)
            nc.vector.tensor_tensor(coT_lo[:, h, :], acc[2 + h % 2][:], coT_hi[:, h, :].bitcast(F32), ALU.subtract).then_inc(co_lo, 1)

        cross_max(0)
        cross_normalize(0)
        cross_max(1)
        for h in range(CH):
            dve.wait_ge(cT_full, 2 * h + 2)
            nc.vector.tensor_copy(probT[1][:], aux[3][:]).then_inc(cT_dve, 1)
            if h + 2 < CH:
                cross_max(h + 2)
            if h:
                cross_output_lo(h - 1)
            if h + 1 < CH:
                cross_normalize(h + 1)
        cross_output_lo(CH - 1)

        def mlp_input_lo(k):
            transposed_lo(k, x2T_hi, aux[k % 4][:], act_lo[:, k, :], act_hi[:, k, :], V_MLP, x2T_lo)

        for j in range(4):
            split(G_CO + j + 1)
            for m in range(4):
                if j:
                    mlp_input_lo(4 * (j - 1) + m)
                wait_bank(dve, B_CO + j, m, G_CO + j)
                nc.vector.tensor_tensor(xs[:, m, cols(j, BLK)], acc[m][:], xs[:, m, cols(j, BLK)], ALU.add).then_inc(bank_free[m], 1)

        def mlp_scale():
            dve.wait_ge(x2_sq, 16)
            step(nc.vector.reduce_sum(m_sum[:], x_sums[:], AX))
            step(nc.vector.tensor_scalar(m_var[:], m_sum[:], 1.0 / D, EPS, ALU.mult, ALU.add))
            step(nc.vector.reciprocal(m_inv[:], m_var[:]))

        def hidden_lo(i, k):
            dve.wait_ge(hid_hi, i * FF_TILES + (k + 1))
            nc.vector.tensor_tensor(br_lo[:, k, :], sq_t[k % 2][:], br_hi[:, k, :].bitcast(F32), ALU.subtract).then_inc(hid_lo, 1)

        def ff_chunk(i, first=False, last=False):
            for j in range(2):
                for g in range(4):
                    split(G_FF + 4 * j + g + 1, i, FF_GR)
                    if first and (j, g) == (0, 0):
                        for k in range(12, KD):
                            mlp_input_lo(k)
                        mlp_scale()
                for k in range(4 * j, 4 * j + 4):
                    if k >= 2:
                        dve.wait_ge(hid_lo, i * FF_TILES + (k - 1))
                    dve.wait_ge(relu_ready, i * FF_TILES + (k + 1))
                    nc.vector.tensor_tensor(sq_t[k % 2][:], relu_t[k % 2][:], acc[k % 4][:], ALU.mult).then_inc(bank_free[k % 4], 1)
                    if k % 4:
                        hidden_lo(i, k - 1)
                hidden_lo(i, 4 * j + 3)
            for j in range(4):
                for g in range(2):
                    if not (last and (j, g) == (3, 1)):
                        split(G_FF + 8 + 2 * j + g + 1, i, FF_GR)
                for m in range(4):
                    if m < 3:
                        wait_bank(dve, B_FF + 2 + j, m, 0, i * FF_BLK)
                    else:
                        dve.wait_ge(granule_used, i * FF_GR + (G_FF + 8 + 2 * j + 2))
                    nc.vector.scalar_tensor_tensor(out=xs[:, m, cols(j, BLK)], in0=acc[m][:], scalar=m_inv[:, m:m + 1],
                                                   in1=xs[:, m, cols(j, BLK)], op0=ALU.mult, op1=ALU.add).then_inc(bank_free[m], 1)
                    if last and j == 3:
                        if m:
                            final_scale(m - 1)
                        final_sum(m)
                if last and j == 0:
                    dve.wait_ge(fin_loaded, 16)
                if last and j < 3:
                    for m in range(4):
                        final_gain(m, j)

        def final_gain(m, j):
            dve.wait_ge(x3_sq, (N_FF - 1) * 16 + 4 * j + m + 1)
            ins = nc.vector.tensor_tensor(xs[:, m, cols(j, BLK)], xs[:, m, cols(j, BLK)], gain_f[:, cols(j, BLK)], ALU.mult)
            if j == 3:
                step(ins)

        def final_sum(m):
            dve.wait_ge(x3_sq, (N_FF - 1) * 16 + 12 + m + 1)
            nc.vector.reduce_sum(f_sum[:, m:m + 1], x_sums[:, m, :], AX).then_inc(f_stat, 1)
            final_gain(m, 3)

        def final_scale(m):
            dve.wait_ge(f_rs_ok, m + 1)
            for half in range(2):
                piece = xs[:, m, cols(half, D // 2)]
                nc.vector.tensor_scalar(piece, piece, f_rs[:, m:m + 1], None, ALU.mult).then_inc(out_ready, 1)

        ff_chunk(0, first=True)
        with dve.Fori(1, N_FF - 1) as i:
            ff_chunk(i)
        ff_chunk(N_FF - 1, last=True)
        final_scale(NT - 1)

    @block.tensor
    def _(pe):
        def product(blk, n, granules, operands, turn=0, blk_per=1, n_per=0, banks=4, width=BLK, hooks=None, inputs=None,
                    tile_input=None):
            hooks = hooks or {}
            for g in range(granules):
                for piece in hooks.get((g, 0), ()):
                    piece()
                if inputs:
                    inputs(g)
                pe.wait_ge(hi_ready, turn * n_per + (n + g + 1))
                pe.wait_ge(lo_ready, turn * n_per + (n + g + 1))
                slot = (n + g) % 2
                for m in range(banks):
                    if g == 0 and blk + m > 0 and uses_before(blk, m) > 0:
                        pe.wait_ge(bank_free[m], turn * blk_per + uses_before(blk, m))
                    for k in range(GR):
                        if tile_input:
                            tile_input(m, GR * g + k)
                        s_hi, s_lo, v_hi, v_lo = operands(m, GR * g + k, slot, k)
                        first, last = g == 0 and k == 0, g == granules - 1 and k == GR - 1
                        dst = acc[m][:, 0:width]
                        nc.tensor.matmul(dst, s_hi, v_hi, start=first, stop=False)
                        nc.tensor.matmul(dst, s_hi, v_lo, start=False, stop=False)
                        ins = nc.tensor.matmul(dst, s_lo, v_hi, start=False, stop=last)
                    if m == banks - 1:
                        ins.then_inc(granule_used, 1)
                    elif g == granules - 1:
                        ins.then_inc(bank_full, 1)
                    for piece in hooks.get((g, m + 1), ()):
                        piece()

        def features(a_hi, a_lo):
            return lambda m, k, s, i: (whi[s][:, i, cols(m)], wlo[s][:, i, cols(m)], a_hi[:, k, :], a_lo[:, k, :])

        def tokens(a_hi, a_lo):
            return lambda m, k, s, i: (a_hi[:, k, cols(m)], a_lo[:, k, cols(m)], whi[s][:, i, :], wlo[s][:, i, :])

        def transposes(src, tiles, k, full):
            for t in range(tiles):
                ins = nc.tensor.transpose(aux[k % 4][:, cols(t)], src[:, t, cols(k)], ident[:])
            ins.then_inc(full, 1)

        pe.wait_ge(vec_loaded, 8 * 16)
        pe.wait_ge(pool_const, 1)
        nc.tensor.transpose(aux[3][:, 0:N_VEC], vec_rows[0:N_VEC, :], ident[0:N_VEC, 0:N_VEC]).then_inc(vec_full, 1)
        for t in range(MT):
            pe.wait_ge(m_loaded[t], 16)

        def memory_tile(k):
            def piece():
                if k == 3:
                    pe.wait_ge(vec_ready, 1)
                if k >= 4:
                    pe.wait_ge(memT_hi_ok, k - 3)
                    pe.wait_ge(memT_lo_ok, k - 3)
                transposes(mem_sb, MT, k, memT_full)
            return piece

        def memory_scales():
            pe.wait_ge(rs_diag_ok, MT)
            pe.wait_ge(pool_const, 2)
            pe.wait_ge(memT_hi_ok, KD - 3)
            pe.wait_ge(memT_lo_ok, KD - 3)
            nc.tensor.matmul(aux[0][:, 0:MEM], ones[:], rs_diag[:], start=True, stop=True).then_inc(rs_row_full, 1)

        for k in range(8):
            memory_tile(k)()

        def memory_input(g):
            pe.wait_ge(memT_hi_ok, GR * g + GR)
            pe.wait_ge(memT_lo_ok, GR * g + GR)

        hooks = {(k // 4 - 2, k % 4 + 1): [memory_tile(k)] for k in range(8, KD)}
        hooks[2, 1] = [memory_scales]
        product(B_CKV, G_CKV, 4, features(memT_hi, memT_lo), width=MEM, inputs=memory_input, hooks=hooks)

        def mixer_input(k):
            def piece():
                pe.wait_ge(x_scaled, NT)
                if k == 0:
                    pe.wait_ge(rs_row_ok, 1)
                if k >= 4:
                    pe.wait_ge(xT_hi_ok, k - 3)
                    pe.wait_ge(xT_lo_ok, k - 3)
                transposes(xs, NT, k, xT_full)
            return piece

        product(B_CKV + 1, G_CKV + 4, 4, tokens(memT_hi, memT_lo), banks=MT,
                hooks={(g, p): [mixer_input(4 * g + 2 * p), mixer_input(4 * g + 2 * p + 1)] for g in range(4) for p in range(2)})
        pe.wait_ge(xT_hi_ok, KD)
        pe.wait_ge(xT_lo_ok, KD)

        mixer = (act_hi, act_lo)
        with pe.Fori(0, 4) as i:
            product(B_QK, G_QK, 4, features(*mixer), turn=i, n_per=4)
        pe.wait_ge(lam_val, 1)
        nc.tensor.matmul(aux[0][:, 0:1], ones[0:1, :], lam_s[0:1, 1:2], start=True, stop=True).then_inc(lam_full, 1)
        with pe.Fori(0, 2) as i:
            product(B_V, G_V, 4, tokens(*mixer), turn=i, n_per=4)

        def head_pieces(h):
            def scores(g):
                def piece():
                    n = (g + 1) * P
                    if g == 0:
                        pe.wait_ge(qk_ready, h + 1)
                    for mp in range(2):
                        half = slice(mp * QK, (mp + 1) * QK)
                        nc.tensor.matmul(aux[mp][:, 0:n], q_map[:, mp, cols(g)], k_map[:, mp, 0:n], start=True, stop=False)
                        ins = nc.tensor.matmul(aux[mp][:, 0:n], q_map[half, mp, cols(g)], k_lo[half, 0:n],
                                               start=False, stop=True)
                    ins.then_inc(scores_full, 1)
                return piece

            def mix_transposes(g):
                def piece():
                    pe.wait_ge(mix_ready, h * NT + (g + 1))
                    for t in range(g + 1):
                        ins = nc.tensor.transpose(aux[2][:, cols(t)], wmix[:, cols(t)], ident[:])
                    ins.then_inc(mixT_full, 1)
                return piece

            def values(g):
                def piece():
                    pe.wait_ge(mixT_ready, h * NT + (g + 1))
                    for t in range(g + 1):
                        ins = nc.tensor.matmul(aux[3][:, 0:P], wmixT[:, cols(t)], av[:, t, ds(h * P, P)],
                                               start=t == 0, stop=t == g)
                    ins.then_inc(att_full, 1)
                return piece

            def output_transpose(g):
                def piece():
                    pe.wait_ge(att_scaled, h * NT + (g + 1))
                    nc.tensor.transpose(aux[3][:, P:2 * P], o_sb[:], ident[:]).then_inc(attT_full, 1)
                return piece

            hooks = {(0, 1): [scores(0)], (0, 3): [mix_transposes(0)], (0, 4): [values(0)], (1, 1): [output_transpose(0)]}
            for g in range(1, NT):
                hooks[g, 0] = [scores(g)]
                hooks[g, 2] = [mix_transposes(g)]
                hooks[g, 3] = [values(g)]
                hooks[g, 4] = [output_transpose(g)]
            return hooks

        pe.wait_ge(neg_lam_ok, 1)
        with pe.Fori(0, HEADS) as h:
            product(B_GATE, G_GATE, 4, features(*mixer), turn=h, n_per=4, hooks=head_pieces(h))

        pe.wait_ge(wif_hi_ok, 1)
        pe.wait_ge(wif_lo_ok, 1)
        for k in range(KD):
            nc.tensor.matmul(aux[0][0:4 * MH, :], wif_parts[:, k, :], act_hi[:, k, :], start=k == 0, stop=False)
            ins = nc.tensor.matmul(aux[0][0:4 * MH, :], wif_parts[:, k, :], act_lo[:, k, :], start=False, stop=k == KD - 1)
        ins.then_inc(if_full, 1)

        def if_transposes():
            pe.wait_ge(ifT_ready, 1)
            for t in range(NT):
                ins = nc.tensor.transpose(aux[1][:, cols(t, 4 * MH)], ifT[:, cols(t)], ident[0:4 * MH, 0:4 * MH])
            ins.then_inc(if_cols_full, 1)

        def cumulate():
            pe.wait_ge(logf_ready, 1)
            pe.wait_ge(pool_const, 3)
            nc.tensor.matmul(aux[1][:, 0:NG], tri[:], gate_col["logf"][:], start=True, stop=True)
            nc.tensor.matmul(aux[1][:, NG:2 * NG], ones[:], gate_col["logf"][:], start=True, stop=True).then_inc(cum_full, 1)

        def u_transpose():
            pe.wait_ge(u_ready, 1)
            nc.tensor.transpose(aux[2][0:NG, 0:P], gate_col["u"][:], ident[:]).then_inc(uT_full, 1)

        def maxima():
            pe.wait_ge(cm_ready, 1)
            nc.tensor.matmul(aux[2][:, P:P + NG], ones[0:NG, :], diag_cm[:], start=True, stop=True)
            nc.tensor.transpose(aux[2][:, P + NG:P + 2 * NG], cmT[:], ident[0:NG, 0:NG]).then_inc(cm_full, 1)

        product(B_MO, G_MO, 4, features(*mixer), hooks={(0, 1): [if_transposes], (1, 1): [cumulate], (2, 1): [u_transpose], (3, 1): [maxima]})
        product(B_MO + 1, G_MO + 4, 4, features(*mixer))
        with pe.Fori(0, 2) as i:
            product(B_MQK, G_MQK, 4, features(*mixer), turn=i, n_per=4)
        with pe.Fori(0, 2) as i:
            product(B_MV, G_MV, 4, tokens(*mixer), turn=i, n_per=4)

        def unit_inner(u):
            c, h = divmod(u, MH)

            def piece():
                pe.wait_ge(diag_ready, u + 1)
                if u >= 2:
                    pe.wait_ge(hm_ready, 2 * (u - 1))
                q, k = mqkT[:, h, cols(c)], mqkT[:, MH + h, cols(c)]
                nc.tensor.matmul(aux[0][:, 0:P], ones[:], diag[:], start=True, stop=True)
                nc.tensor.matmul(aux[0][:, P:2 * P], k, q, start=True, stop=True)
                nc.tensor.transpose(aux[0][:, 2 * P:3 * P], k, ident[:]).then_inc(dqk_full, 1)
            return piece

        def unit_outer(u):
            c, h = divmod(u, MH)

            def piece():
                if c:
                    pe.wait_ge(c_ready, u - MH + 1)
                    nc.tensor.matmul(aux[1][:, 0:MV + 1], mqkT[:, h, cols(c)], state[:, h, :], start=True, stop=True)
                if u == 0:
                    pe.wait_ge(vaug_ones, 1)
                    pe.wait_ge(bank_free[3], freed(B_MV + 1, 3))
                pe.wait_ge(w_ready, u + 1)
                nc.tensor.matmul(aux[2][:, 0:MV + 1], ew[:], vaug[:, c, h, :], start=True, stop=True).then_inc(n_full, 1)
                if c == NT - 1:
                    return
                if u:
                    pe.wait_ge(hm_ready, 2 * u)
                nc.tensor.matmul(aux[3][:, 0:MV + 1], kw[:], vaug[:, c, h, :], start=True, stop=True).then_inc(c_full, 1)
            return piece

        def unit_transposes(u):
            def piece():
                pe.wait_ge(h_ready, u + 1)
                pe.wait_ge(w_ready, min(u + 2, NG))
                nc.tensor.transpose(aux[0][:, 3 * P:4 * P], num[:, 0:P], ident[:])
                nc.tensor.transpose(aux[3][:, 3 * P:4 * P], num[:, P:2 * P], ident[:]).then_inc(hT_full, 1)
            return piece

        pe.wait_ge(mqk_ready, 2 * MH)
        pe.wait_ge(att_hi, HEADS)
        pe.wait_ge(att_lo, HEADS)
        unit_inner(0)()
        for j in range(4):
            hooks = {}
            for g in range(2):
                a = 4 * j + 2 * g
                hooks[g, 1] = ([unit_transposes(a - 1)] if a else []) + [unit_outer(a), unit_inner(a + 1)]
                hooks[g, 3] = [unit_transposes(a), unit_outer(a + 1)] + ([unit_inner(a + 2)] if a + 2 < NG else [])
            product(B_ABR + j, G_ABR + 2 * j, 2, features(br_hi, br_lo), hooks=hooks)

        def waits(hi, lo, turn=0, per=0):
            def inputs(g):
                pe.wait_ge(hi, turn * per + GR * (g + 1))
                pe.wait_ge(lo, turn * per + GR * (g + 1))
            return inputs

        for j in range(4):
            product(B_MBR + j, G_MBR + 2 * j, 2, features(br_hi, br_lo), inputs=waits(hm_hi, hm_lo),
                    hooks={} if j else {(0, 1): [unit_transposes(NG - 1)]})
        with pe.Fori(0, 3) as i:
            product(B_OUT, G_OUT, 4, tokens(act_hi, act_lo), turn=i, n_per=4, inputs=waits(y_hi, y_lo))

        def residual_transposes(k, blk, full, hi, lo):
            def piece():
                for m in range(4):
                    pe.wait_ge(bank_free[m], freed(blk + k // 4, m))
                if k >= 4:
                    pe.wait_ge(hi, k - 3)
                    pe.wait_ge(lo, k - 3)
                transposes(xs, NT, k, full)
            return piece

        def x1_tile(k):
            return residual_transposes(k, B_OUT, x1T_full, x1T_hi, x1T_lo)

        product(B_OUT + 3, G_OUT + 12, 4, tokens(act_hi, act_lo), inputs=waits(y_hi, y_lo),
                hooks={(2 + k // 4, k % 4 + 1): [x1_tile(k)] for k in range(8)})

        def cross_scores(h):
            pe.wait_ge(bank_free[h], freed(B_CQ, h))
            if h == 0:
                pe.wait_ge(x1T_lo, KD)
            if h == 1:
                pe.wait_ge(bank_free[0], freed(B_CQ, 0))
            if h >= 2:
                pe.wait_ge(cexp_ready, NT * (h - 1))
            for t in range(NT):
                ins = nc.tensor.matmul(score_bank(h, t // 2)[:, cols(t % 2, MEM)], cqT[:, h, cols(t)], ckT[:, h, :],
                                       start=True, stop=True)
                if t % 2:
                    ins.then_inc(cs_full, 1)

        hooks = {(k // 4 - 2, k % 4 + 1): [x1_tile(k)] for k in range(8, KD)}
        hooks[3, 2] = [lambda: cross_scores(0)]
        hooks[3, 4] = [lambda: cross_scores(1)]
        product(B_CQ, G_CQ, 4, features(act_hi, act_lo), inputs=waits(x1T_hi, x1T_lo), hooks=hooks)
        for h in range(CH):
            for half in range(MT):
                pe.wait_ge(cprob_ready, NT * (h + 1))
                for t in range(NT):
                    ins = nc.tensor.transpose(aux[2 + half][:, cols(t)], cprob[h % 2][:, t, cols(half)], ident[:])
                ins.then_inc(cT_full, 1)
            if h + 2 < CH:
                cross_scores(h + 2)
            pe.wait_ge(cT_act, h + 1)
            if h >= 2:
                pe.wait_ge(co_lo, h - 1)
            nc.tensor.matmul(acc[2 + h % 2][:], cv[:, 0, cols(h)], probT[0][:], start=True, stop=False)
            pe.wait_ge(cT_dve, h + 1)
            nc.tensor.matmul(acc[2 + h % 2][:], cv[:, 1, cols(h)], probT[1][:], start=False, stop=True).then_inc(co_full, 1)

        def x2_tile(k):
            return residual_transposes(k, B_CO, x2T_full, x2T_hi, x2T_lo)

        def x2_tiles(j):
            return {(0, 2): [x2_tile(4 * j)], (0, 3): [x2_tile(4 * j + 1)], (0, 4): [x2_tile(4 * j + 2), x2_tile(4 * j + 3)]}

        def head_output(m, h):
            if m == 0:
                pe.wait_ge(co_lo, h + 1)

        pe.wait_ge(cexp_ready, NT * CH)
        for j in range(4):
            hooks = x2_tiles(j - 1) if j else {}
            product(B_CO + j, G_CO + j, 1, tokens(coT_hi, coT_lo), hooks=hooks, tile_input=None if j else head_output)

        def ff_chunk(i, first=False):
            for j in range(2):
                product(B_FF + j, G_FF + 4 * j, 4, features(act_hi, act_lo), turn=i, blk_per=FF_BLK, n_per=FF_GR,
                        inputs=waits(x2T_hi, x2T_lo), hooks=x2_tiles(3) if first and j == 0 else {})
            for j in range(4):
                product(B_FF + 2 + j, G_FF + 8 + 2 * j, 2, tokens(br_hi, br_lo), turn=i, blk_per=FF_BLK, n_per=FF_GR,
                        inputs=waits(hid_hi, hid_lo, i, FF_TILES))

        ff_chunk(0, first=True)
        with pe.Fori(1, N_FF) as i:
            ff_chunk(i)

    ctx.close()


_INS = ["x", "mem", "norm_mix", "w_in", "b_igate", "b_fgate", "conv_w", "conv_b", "lam_q1", "lam_k1", "lam_q2", "lam_k2",
        "attn_norm", "mlstm_norm", "w_attn_br", "w_mlstm_br", "w_out", "norm_cross", "norm_mem", "w_cq", "w_ckv", "w_co",
        "norm_mlp", "w_up", "w_down", "norm_final"]


def kernel(**inputs):
    import concourse.bacc as bacc
    from concourse.bass_utils import run_bass_kernel_spmd

    nc = bacc.Bacc("TRN2", target_bir_lowering=False, num_devices=1, dynamic_dma_scratch_size=1024)
    arrays, args = {}, []
    for name in _INS:
        a = np.ascontiguousarray(inputs[name])
        arrays[f"in_{name}"] = a
        args.append(nc.dram_tensor(f"in_{name}", a.shape, mybir.dt.from_np(a.dtype), kind="ExternalInput").ap())
    args.append(nc.dram_tensor("out_0", (1, SEQ, D), F32, kind="ExternalOutput").ap())
    hybrid_layer(nc, *args)
    r = run_bass_kernel_spmd(nc, [arrays], core_ids=[0])
    return r.results[0]["out_0"]
```
